# Optimizing a Trainium2 kernel written in Bass

```python
import math
import jax, jax.numpy as jnp
from jax import lax
import numpy as np

D_MODEL = 1024
BATCH = 1
SEQ = 256
DEPTH = 1

HEAD_DIM = 128
HEADS_PER_GROUP = 4
DILATED_GROUPS = ((128, 1), (512, 4), (2048, 16))
N_GROUPS = 3
N_ATTN_HEADS = N_GROUPS * HEADS_PER_GROUP
ATTN_QKV_WIDTH = N_ATTN_HEADS * HEAD_DIM
ATTN_OUT_WIDTH = HEADS_PER_GROUP * HEAD_DIM
BAND_BLOCK = 128
LRU_WIDTH = D_MODEL
LRU_HEADS = 4
LRU_HEAD_DIM = LRU_WIDTH // LRU_HEADS
CONV_WIDTH = 4
LRU_C = 8.0
D_FF = 2816
REL_BUCKETS = 32
REL_MAX_DISTANCE = 2048
NORM_EPS = 1e-6
N_BRANCHES = 2
W_IN_COLS = 3 * ATTN_QKV_WIDTH + 2 * LRU_WIDTH + N_BRANCHES * D_MODEL


def rms_norm(x, g):
    xf = x.astype(jnp.float32)
    y = xf * lax.rsqrt(jnp.mean(xf * xf, axis=-1, keepdims=True) + NORM_EPS)
    return (y * g.astype(jnp.float32)).astype(x.dtype)

def swiglu(x, w_gate, w_up, w_down):
    return (jax.nn.silu(x @ w_gate) * (x @ w_up)) @ w_down

def t5_causal_bucket(distance):
    max_exact = REL_BUCKETS // 2
    nf = jnp.maximum(distance, 1).astype(jnp.float32)
    large = max_exact + (jnp.log(nf / max_exact) / math.log(REL_MAX_DISTANCE / max_exact)
                         * (REL_BUCKETS - max_exact)).astype(jnp.int32)
    large = jnp.minimum(large, REL_BUCKETS - 1)
    return jnp.where(distance < max_exact, distance, large)

def dilated_group_attention(q, k, v, bias_table_g, window, dilation):
    B, S, H, E = q.shape
    d = dilation
    L = S // d
    nb = -(-L // BAND_BLOCK)
    Lp = nb * BAND_BLOCK
    m_max = window // d

    def to_blocks(t):
        t = t.reshape(B, L, d, H, E)
        t = jnp.pad(t, ((0, 0), (0, Lp - L), (0, 0), (0, 0), (0, 0)))
        return t.reshape(B, nb, BAND_BLOCK, d, H, E)

    def band(t):
        tb = jnp.pad(to_blocks(t), ((0, 0), (1, 0), (0, 0), (0, 0), (0, 0), (0, 0)))
        return jnp.concatenate([tb[:, :-1], tb[:, 1:]], axis=2)

    qb = to_blocks(q)
    kb = band(k)
    vb = band(v)

    qi = jnp.arange(BAND_BLOCK)[:, None]
    kj = jnp.arange(2 * BAND_BLOCK)[None, :]
    steps = qi + BAND_BLOCK - kj
    key_idx = jnp.arange(nb)[:, None, None] * BAND_BLOCK - BAND_BLOCK + kj[None]
    valid = (steps >= 0) & (steps <= m_max) & (key_idx >= 0)
    bucket = t5_causal_bucket(jnp.maximum(steps, 0) * d)
    bias = jnp.transpose(bias_table_g[bucket], (2, 0, 1)).astype(jnp.float32)

    scale = 1.0 / math.sqrt(E)
    scores = jnp.einsum('bnqphe,bnkphe->bphnqk', qb, kb).astype(jnp.float32) * scale
    scores = scores + bias[None, None, :, None]
    scores = jnp.where(valid[None, None, None], scores, -jnp.inf)
    mx = jnp.max(scores, axis=-1, keepdims=True)
    e = jnp.exp(scores - mx)
    den = jnp.sum(e, axis=-1, keepdims=True)
    o = jnp.einsum('bphnqk,bnkphe->bnqphe', (e / den).astype(v.dtype), vb)
    lse = (mx + jnp.log(den))[..., 0]
    o = o.reshape(B, Lp, d, H, E)[:, :L].reshape(B, S, H, E)
    lse = jnp.transpose(lse, (0, 3, 4, 1, 2)).reshape(B, Lp, d, H)[:, :L].reshape(B, S, H)
    return o, lse

def rg_lru_branch(xr, conv_w, conv_b, w_x, b_x, w_a, b_a, a_param):
    B, S, C = xr.shape
    xc = lax.conv_general_dilated(
        xr, conv_w[:, None, :].astype(xr.dtype), window_strides=(1,),
        padding=((CONV_WIDTH - 1, 0),), dimension_numbers=('NWC', 'WIO', 'NWC'),
        feature_group_count=C) + conv_b
    xh = xc.reshape(B, S, LRU_HEADS, LRU_HEAD_DIM)
    gate_x = jax.nn.sigmoid(jnp.einsum('bshi,hij->bshj', xh, w_x) + b_x).reshape(B, S, C)
    gate_a = jax.nn.sigmoid(jnp.einsum('bshi,hij->bshj', xh, w_a) + b_a).reshape(B, S, C)
    log_a = -LRU_C * gate_a.astype(jnp.float32) * jax.nn.softplus(-a_param.astype(jnp.float32))
    a = jnp.exp(log_a)
    b = jnp.sqrt(-jnp.expm1(2.0 * log_a)) * (gate_x * xc).astype(jnp.float32)

    def combine(left, right):
        a_l, b_l = left
        a_r, b_r = right
        return a_l * a_r, a_r * b_l + b_r

    _, h = lax.associative_scan(combine, (a, b), axis=1)
    return h.astype(xr.dtype)

def first_inputs(seed: int = 0) -> dict:
    key = jax.random.key(seed)
    ks = jax.random.split(key, 32)
    f32 = jnp.float32

    def w(k, shape, fan_in):
        return jax.random.normal(k, shape, f32) * (fan_in ** -0.5)

    def gain(k):
        return 1.0 + 0.05 * jax.random.normal(k, (DEPTH, D_MODEL), f32)

    a0 = jax.random.uniform(ks[20], (DEPTH, LRU_WIDTH), f32, 0.9, 0.999)
    s = a0 ** (1.0 / LRU_C)
    a_param = jnp.log(s) - jnp.log1p(-s)

    return {
        "x": jax.random.normal(ks[0], (BATCH, SEQ, D_MODEL), f32),
        "ffn1_norm_pre": gain(ks[1]),
        "ffn1_norm_post": gain(ks[2]),
        "ffn1_w_gate": w(ks[3], (DEPTH, D_MODEL, D_FF), D_MODEL),
        "ffn1_w_up": w(ks[4], (DEPTH, D_MODEL, D_FF), D_MODEL),
        "ffn1_w_down": w(ks[5], (DEPTH, D_FF, D_MODEL), D_FF),
        "mix_norm_pre": gain(ks[6]),
        "mix_norm_post": gain(ks[7]),
        "w_in": w(ks[8], (DEPTH, D_MODEL, W_IN_COLS), D_MODEL),
        "rel_bias_table": 0.2 * jax.random.normal(ks[9], (REL_BUCKETS, N_ATTN_HEADS), f32),
        "conv_w": w(ks[10], (DEPTH, CONV_WIDTH, LRU_WIDTH), CONV_WIDTH),
        "conv_b": 0.02 * jax.random.normal(ks[11], (DEPTH, LRU_WIDTH), f32),
        "lru_w_x": w(ks[12], (DEPTH, LRU_HEADS, LRU_HEAD_DIM, LRU_HEAD_DIM), LRU_HEAD_DIM),
        "lru_b_x": 0.02 * jax.random.normal(ks[13], (DEPTH, LRU_HEADS, LRU_HEAD_DIM), f32),
        "lru_w_a": w(ks[14], (DEPTH, LRU_HEADS, LRU_HEAD_DIM, LRU_HEAD_DIM), LRU_HEAD_DIM),
        "lru_b_a": 0.02 * jax.random.normal(ks[15], (DEPTH, LRU_HEADS, LRU_HEAD_DIM), f32),
        "lru_a_param": a_param,
        "w_attn_branch": w(ks[16], (DEPTH, ATTN_OUT_WIDTH, D_MODEL), ATTN_OUT_WIDTH),
        "w_rec_branch": w(ks[17], (DEPTH, LRU_WIDTH, D_MODEL), LRU_WIDTH),
        "w_out": w(ks[18], (DEPTH, D_MODEL, D_MODEL), D_MODEL),
        "ffn2_norm_pre": gain(ks[21]),
        "ffn2_norm_post": gain(ks[22]),
        "ffn2_w_gate": w(ks[23], (DEPTH, D_MODEL, D_FF), D_MODEL),
        "ffn2_w_up": w(ks[24], (DEPTH, D_MODEL, D_FF), D_MODEL),
        "ffn2_w_down": w(ks[25], (DEPTH, D_FF, D_MODEL), D_FF),
    }

def first_block(x, ffn1_norm_pre, ffn1_norm_post, ffn1_w_gate, ffn1_w_up, ffn1_w_down,
              mix_norm_pre, mix_norm_post, w_in, rel_bias_table, conv_w, conv_b,
              lru_w_x, lru_b_x, lru_w_a, lru_b_a, lru_a_param,
              w_attn_branch, w_rec_branch, w_out,
              ffn2_norm_pre, ffn2_norm_post, ffn2_w_gate, ffn2_w_up, ffn2_w_down):
    B, S, _ = x.shape
    splits = [ATTN_QKV_WIDTH, 2 * ATTN_QKV_WIDTH, 3 * ATTN_QKV_WIDTH,
              3 * ATTN_QKV_WIDTH + LRU_WIDTH, 3 * ATTN_QKV_WIDTH + 2 * LRU_WIDTH]
    h = x
    for l in range(DEPTH):
        f = swiglu(rms_norm(h, ffn1_norm_pre[l]), ffn1_w_gate[l], ffn1_w_up[l], ffn1_w_down[l])
        h = h + 0.5 * rms_norm(f, ffn1_norm_post[l])

        u = rms_norm(h, mix_norm_pre[l])
        proj = u @ w_in[l]
        q, k, v, xr, yr, gl = jnp.split(proj, splits, axis=-1)
        q = q.reshape(B, S, N_GROUPS, HEADS_PER_GROUP, HEAD_DIM)
        k = k.reshape(B, S, N_GROUPS, HEADS_PER_GROUP, HEAD_DIM)
        v = v.reshape(B, S, N_GROUPS, HEADS_PER_GROUP, HEAD_DIM)

        outs, lses = [], []
        for g, (window, dilation) in enumerate(DILATED_GROUPS):
            o_g, lse_g = dilated_group_attention(
                q[:, :, g], k[:, :, g], v[:, :, g],
                rel_bias_table[:, g * HEADS_PER_GROUP:(g + 1) * HEADS_PER_GROUP],
                window, dilation)
            outs.append(o_g)
            lses.append(lse_g)
        alpha = jax.nn.softmax(jnp.stack(lses, axis=0), axis=0)
        attn = jnp.einsum('gbsh,gbshe->bshe', alpha, jnp.stack(outs, axis=0).astype(jnp.float32))
        attn_d = attn.astype(x.dtype).reshape(B, S, ATTN_OUT_WIDTH) @ w_attn_branch[l]

        rec = rg_lru_branch(xr, conv_w[l], conv_b[l], lru_w_x[l], lru_b_x[l],
                            lru_w_a[l], lru_b_a[l], lru_a_param[l]) * jax.nn.gelu(yr)
        rec_d = rec @ w_rec_branch[l]

        gates = jax.nn.sigmoid(gl).reshape(B, S, N_BRANCHES, D_MODEL)
        merged = gates[:, :, 0] * attn_d + gates[:, :, 1] * rec_d
        h = h + rms_norm(merged @ w_out[l], mix_norm_post[l])

        f = swiglu(rms_norm(h, ffn2_norm_pre[l]), ffn2_w_gate[l], ffn2_w_up[l], ffn2_w_down[l])
        h = h + 0.5 * rms_norm(f, ffn2_norm_post[l])
    return h


GRID_W = 64
CTX_LEN = 256
MIX_WIDTH = D_MODEL
RWKV_WIDTH = MIX_WIDTH // 2
HEAD_SIZE = 64
RWKV_HEADS = RWKV_WIDTH // HEAD_SIZE
FNET_WIDTH = MIX_WIDTH - RWKV_WIDTH
FNET_GROUPS = 8
FNET_GROUP_W = FNET_WIDTH // FNET_GROUPS
DECAY_LORA = 64
ICLR_LORA = 64
GATE_LORA = 128
N_DIR = 2
SHIFT_WIDTH = 3 * RWKV_WIDTH + N_DIR * (DECAY_LORA + ICLR_LORA + GATE_LORA)
IN_WIDTH = SHIFT_WIDTH + FNET_WIDTH
N_EXPERTS = 32
TOP_K = 4
D_FF_2 = D_MODEL
SWIGLU_LIMIT = 7.0
SWIGLU_ALPHA = 1.702
EXPERT_BLOCK = 128
DEEPNORM_ALPHA = (2.0 * DEPTH) ** 0.25
DEEPNORM_BETA = (8.0 * DEPTH) ** -0.25
LN_EPS = 1e-5
GN_EPS = 64e-5


def layer_norm(u, g, b):
    u32 = u.astype(jnp.float32)
    mean = jnp.mean(u32, -1, keepdims=True)
    var = jnp.mean(jnp.square(u32 - mean), -1, keepdims=True)
    return ((u32 - mean) * lax.rsqrt(var + LN_EPS) * g + b).astype(u.dtype)

def grid_shift(u):
    b_, t, ch = u.shape
    rows = t // GRID_W
    g = u.reshape(b_, rows, GRID_W, ch)
    p = jnp.pad(g, ((0, 0), (1, 1), (1, 1), (0, 0)))
    nb = (p[:, :-2, 1:-1] + p[:, 2:, 1:-1] + p[:, 1:-1, :-2] + p[:, 1:-1, 2:]) * 0.25
    return nb.reshape(b_, t, ch)

def seq_shift(u):
    p = jnp.pad(u, ((0, 0), (1, 1), (0, 0)))
    return (p[:, :-2] + p[:, 2:]) * 0.5

def heads(z):
    return z.reshape(z.shape[:-1] + (RWKV_HEADS, HEAD_SIZE))

def rwkv_prepare(m, w0, w2_decay, a0, a2_iclr, g2_gate, k_k, k_a):
    b_, t, _ = m.shape
    c = RWKV_WIDTH
    r = m[..., :c]
    k = m[..., c:2 * c]
    v = m[..., 2 * c:3 * c]
    o = 3 * c
    wd = m[..., o:o + N_DIR * DECAY_LORA].reshape(b_, t, N_DIR, DECAY_LORA)
    o += N_DIR * DECAY_LORA
    ad = m[..., o:o + N_DIR * ICLR_LORA].reshape(b_, t, N_DIR, ICLR_LORA)
    o += N_DIR * ICLR_LORA
    gd = m[..., o:o + N_DIR * GATE_LORA].reshape(b_, t, N_DIR, GATE_LORA)
    w_log = w0 + jnp.einsum('btdr,drc->btdc', jnp.tanh(wd), w2_decay)
    w = jnp.exp(-jnp.exp(-jax.nn.softplus(-w_log) - 0.5))
    a = jax.nn.sigmoid(a0 + jnp.einsum('btdr,drc->btdc', ad, a2_iclr))
    g = jnp.einsum('btdr,drc->btdc', jax.nn.sigmoid(gd), g2_gate)
    kk = heads(k * k_k)
    kk = kk / jnp.maximum(jnp.sqrt(jnp.sum(jnp.square(kk), -1, keepdims=True)), 1e-12)
    k_d = k[:, :, None] * (1.0 + (a - 1.0) * k_a)
    return heads(r), heads(k_d), heads(v), kk, heads(w), heads(a), g

def wkv_bidir(r, k_d, v, kk, w, a, state0):
    def both(u):
        return jnp.stack([u, jnp.flip(u, 1)], 0)

    def per(u):
        return jnp.stack([u[:, :, 0], jnp.flip(u[:, :, 1], 1)], 0)

    def tm(z):
        return jnp.moveaxis(z, 2, 0)

    xs = (tm(both(r)), tm(per(w)), tm(per(k_d)), tm(both(v)), tm(both(-kk)), tm(per(kk[:, :, None] * a)))

    def step(s, inp):
        r_t, w_t, k_t, v_t, aa_t, bb_t = inp
        sa = jnp.einsum('dbhij,dbhj->dbhi', s, aa_t)
        s = s * w_t[..., None, :] + sa[..., :, None] * bb_t[..., None, :] + v_t[..., :, None] * k_t[..., None, :]
        y_t = jnp.einsum('dbhij,dbhj->dbhi', s, r_t)
        return s, y_t

    state, ys = lax.scan(step, state0, xs)
    ys = jnp.moveaxis(ys, 0, 2)
    y = jnp.stack([ys[0], jnp.flip(ys[1], 1)], axis=2)
    return y, state

def rwkv_output(y, r, k_d, v, g, r_k, gn_g, gn_b):
    b_, t = y.shape[:2]
    mean = jnp.mean(y, -1, keepdims=True)
    var = jnp.mean(jnp.square(y - mean), -1, keepdims=True)
    yn = (y - mean) * lax.rsqrt(var + GN_EPS) * heads(gn_g) + heads(gn_b)
    bonus = jnp.sum(r[:, :, None] * k_d * r_k, -1, keepdims=True) * v[:, :, None]
    return jnp.sum((yn + bonus).reshape(b_, t, N_DIR, RWKV_WIDTH) * g, axis=2)

def fourier_mix(f, w_fno, b_fno):
    b_, t, _ = f.shape
    fg = f.reshape(b_, t, FNET_GROUPS, FNET_GROUP_W).astype(jnp.float32)
    spec = jnp.real(jnp.fft.fft2(fg, axes=(1, 3), norm='ortho'))
    y = jnp.einsum('btgc,gce->btge', spec, w_fno) + b_fno
    return y.reshape(b_, t, FNET_WIDTH)

def token_mixer(h_lat, h_ctx, w_in, mu_shift, w0, w2_decay, a0, a2_iclr, g2_gate, r_k, k_k, k_a,
                gn_g, gn_b, w_fno, b_fno, w_out, need_ctx):
    f32 = jnp.float32
    p_lat = jnp.einsum('btd,de->bte', h_lat, w_in).astype(f32)
    p_ctx = jnp.einsum('btd,de->bte', h_ctx, w_in).astype(f32)
    s_lat, f_lat = p_lat[..., :SHIFT_WIDTH], p_lat[..., SHIFT_WIDTH:]
    s_ctx, f_ctx = p_ctx[..., :SHIFT_WIDTH], p_ctx[..., SHIFT_WIDTH:]
    mu = mu_shift.astype(f32)
    m_lat = s_lat + mu * (grid_shift(s_lat) - s_lat)
    m_ctx = s_ctx + mu * (seq_shift(s_ctx) - s_ctx)
    dp = (w0, w2_decay, a0, a2_iclr, g2_gate, k_k, k_a)
    r_c, k_c, v_c, kk_c, w_c, a_c, g_c = rwkv_prepare(m_ctx, *dp)
    state0 = jnp.zeros((N_DIR, h_ctx.shape[0], RWKV_HEADS, HEAD_SIZE, HEAD_SIZE), f32)
    y_c, state_c = wkv_bidir(r_c, k_c, v_c, kk_c, w_c, a_c, state0)
    r_l, k_l, v_l, kk_l, w_l, a_l, g_l = rwkv_prepare(m_lat, *dp)
    y_l, _ = wkv_bidir(r_l, k_l, v_l, kk_l, w_l, a_l, state_c)
    rw_lat = rwkv_output(y_l, r_l, k_l, v_l, g_l, r_k, gn_g, gn_b)
    out_lat = jnp.concatenate([rw_lat, fourier_mix(f_lat, w_fno, b_fno)], -1) @ w_out.astype(f32)
    out_ctx = None
    if need_ctx:
        rw_ctx = rwkv_output(y_c, r_c, k_c, v_c, g_c, r_k, gn_g, gn_b)
        out_ctx = (jnp.concatenate([rw_ctx, fourier_mix(f_ctx, w_fno, b_fno)], -1) @ w_out.astype(f32)).astype(h_ctx.dtype)
    return out_lat.astype(h_lat.dtype), out_ctx

def moe_ffn(h, w_router, b_router, w1, b1, w2, b2):
    f32 = jnp.float32
    n_tok = h.shape[0]
    logits = h.astype(f32) @ w_router.astype(f32) + b_router.astype(f32)
    top_val, top_idx = lax.top_k(logits, TOP_K)
    gates = jax.nn.softmax(top_val, axis=-1)
    n_assign = n_tok * TOP_K
    e_flat = top_idx.reshape(-1).astype(jnp.int32)
    tok_flat = jnp.repeat(jnp.arange(n_tok, dtype=jnp.int32), TOP_K)
    g_flat = gates.reshape(-1)
    order = jnp.argsort(e_flat)
    e_s, tok_s, g_s = e_flat[order], tok_flat[order], g_flat[order]
    counts = jnp.bincount(e_flat, length=N_EXPERTS).astype(jnp.int32)
    starts = jnp.cumsum(counts) - counts
    padded = (counts + EXPERT_BLOCK - 1) // EXPERT_BLOCK * EXPERT_BLOCK
    pends = jnp.cumsum(padded)
    pstarts = pends - padded
    slot = pstarts[e_s] + jnp.arange(n_assign, dtype=jnp.int32) - starts[e_s]
    n_blocks = -(-n_assign // EXPERT_BLOCK) + N_EXPERTS
    n_slots = n_blocks * EXPERT_BLOCK
    slot_tok = jnp.zeros((n_slots,), jnp.int32).at[slot].set(tok_s)
    slot_gate = jnp.zeros((n_slots,), f32).at[slot].set(g_s)
    block_start = jnp.arange(n_blocks, dtype=jnp.int32) * EXPERT_BLOCK
    block_e = jnp.minimum(jnp.searchsorted(pends, block_start, side='right'), N_EXPERTS - 1)

    def expert_block(args):
        tok_b, e = args
        xb = h[tok_b]
        u = xb @ w1[e] + b1[e]
        glu = jnp.minimum(u[:, 0::2], SWIGLU_LIMIT)
        lin = jnp.clip(u[:, 1::2], -SWIGLU_LIMIT, SWIGLU_LIMIT)
        act = glu * jax.nn.sigmoid(SWIGLU_ALPHA * glu) * (lin + 1.0)
        return act @ w2[e] + b2[e]

    y = lax.map(expert_block, (slot_tok.reshape(n_blocks, EXPERT_BLOCK), block_e))
    out = jnp.zeros((n_tok, h.shape[1]), f32).at[slot_tok].add(slot_gate[:, None] * y.reshape(n_slots, -1))
    return out.astype(h.dtype)

def second_inputs(seed: int = 0) -> dict:
    key = jax.random.key(seed)
    ks = iter(jax.random.split(key, 48))
    f32 = jnp.float32

    def nrm(shape, scale):
        return scale * jax.random.normal(next(ks), shape, f32)

    L, C, H, N = DEPTH, RWKV_WIDTH, RWKV_HEADS, HEAD_SIZE
    x = nrm((BATCH, SEQ, D_MODEL), 1.0)
    c = nrm((BATCH, D_MODEL), 1.0)
    ctx = nrm((BATCH, CTX_LEN, D_MODEL), 1.0)
    c_ctx = nrm((D_MODEL,), 1.0)
    ln0_g = 1.0 + nrm((D_MODEL,), 0.05)
    ln0_b = nrm((D_MODEL,), 0.02)
    w_ada = nrm((L, D_MODEL, 6 * D_MODEL), 0.5 * D_MODEL ** -0.5)
    b_ada = nrm((L, 6 * D_MODEL), 0.02)
    w_in = nrm((L, D_MODEL, IN_WIDTH), D_MODEL ** -0.5)
    w_in = w_in.at[:, :, 2 * C:3 * C].multiply(DEEPNORM_BETA)
    mu_shift = jax.random.uniform(next(ks), (L, SHIFT_WIDTH), f32, 0.2, 0.8)
    w0 = jax.random.uniform(next(ks), (L, N_DIR, C), f32, -6.0, 1.0)
    w2_decay = nrm((L, N_DIR, DECAY_LORA, C), 0.5 * DECAY_LORA ** -0.5)
    a0 = nrm((L, N_DIR, C), 0.5)
    a2_iclr = nrm((L, N_DIR, ICLR_LORA, C), 0.5 * ICLR_LORA ** -0.5)
    g2_gate = nrm((L, N_DIR, GATE_LORA, C), GATE_LORA ** -0.5)
    r_k = nrm((L, N_DIR, H, N), 0.1)
    k_k = 0.85 + nrm((L, C), 0.05)
    k_a = 1.0 + nrm((L, C), 0.05)
    gn_g = 1.0 + nrm((L, C), 0.05)
    gn_b = nrm((L, C), 0.02)
    w_fno = nrm((L, FNET_GROUPS, FNET_GROUP_W, FNET_GROUP_W), FNET_GROUP_W ** -0.5)
    b_fno = nrm((L, FNET_GROUPS, FNET_GROUP_W), 0.02)
    w_out = nrm((L, MIX_WIDTH, D_MODEL), DEEPNORM_BETA * MIX_WIDTH ** -0.5)
    ln1_g = 1.0 + nrm((L, D_MODEL), 0.05)
    ln1_b = nrm((L, D_MODEL), 0.02)
    w_router = nrm((L, D_MODEL, N_EXPERTS), D_MODEL ** -0.5)
    b_router = nrm((L, N_EXPERTS), 0.01)
    w1 = nrm((L, N_EXPERTS, D_MODEL, 2 * D_FF_2), D_MODEL ** -0.5)
    b1 = nrm((L, N_EXPERTS, 2 * D_FF_2), 0.02)
    w2 = nrm((L, N_EXPERTS, D_FF_2, D_MODEL), DEEPNORM_BETA * D_FF_2 ** -0.5)
    b2 = nrm((L, N_EXPERTS, D_MODEL), 0.02)
    ln2_g = 1.0 + nrm((L, D_MODEL), 0.05)
    ln2_b = nrm((L, D_MODEL), 0.02)
    return {"x": x, "c": c, "ctx": ctx, "c_ctx": c_ctx, "ln0_g": ln0_g, "ln0_b": ln0_b,
            "w_ada": w_ada, "b_ada": b_ada, "w_in": w_in, "mu_shift": mu_shift, "w0": w0,
            "w2_decay": w2_decay, "a0": a0, "a2_iclr": a2_iclr, "g2_gate": g2_gate, "r_k": r_k,
            "k_k": k_k, "k_a": k_a, "gn_g": gn_g, "gn_b": gn_b, "w_fno": w_fno, "b_fno": b_fno,
            "w_out": w_out, "ln1_g": ln1_g, "ln1_b": ln1_b, "w_router": w_router, "b_router": b_router,
            "w1": w1, "b1": b1, "w2": w2, "b2": b2, "ln2_g": ln2_g, "ln2_b": ln2_b}

def second_block(x, c, ctx, c_ctx, ln0_g, ln0_b, w_ada, b_ada, w_in, mu_shift, w0, w2_decay, a0, a2_iclr,
              g2_gate, r_k, k_k, k_a, gn_g, gn_b, w_fno, b_fno, w_out, ln1_g, ln1_b, w_router, b_router,
              w1, b1, w2, b2, ln2_g, ln2_b):
    x = layer_norm(x, ln0_g, ln0_b)
    ctx = layer_norm(ctx, ln0_g, ln0_b)
    for l in range(DEPTH):
        need_ctx = l < DEPTH - 1
        mod = (jax.nn.silu(c) @ w_ada[l] + b_ada[l])[:, None, :]
        sh1, sc1, gt1, sh2, sc2, gt2 = jnp.split(mod, 6, axis=-1)
        mod_c = jax.nn.silu(c_ctx) @ w_ada[l] + b_ada[l]
        sh1c, sc1c, gt1c, sh2c, sc2c, gt2c = jnp.split(mod_c, 6, axis=-1)
        h = x * (1.0 + sc1) + sh1
        hc = ctx * (1.0 + sc1c) + sh1c
        mo, mo_c = token_mixer(h, hc, w_in[l], mu_shift[l], w0[l], w2_decay[l], a0[l], a2_iclr[l], g2_gate[l],
                               r_k[l], k_k[l], k_a[l], gn_g[l], gn_b[l], w_fno[l], b_fno[l], w_out[l], need_ctx)
        x = layer_norm(DEEPNORM_ALPHA * x + gt1 * mo, ln1_g[l], ln1_b[l])
        h = x * (1.0 + sc2) + sh2
        f = moe_ffn(h.reshape(-1, D_MODEL), w_router[l], b_router[l], w1[l], b1[l], w2[l], b2[l]).reshape(x.shape)
        x = layer_norm(DEEPNORM_ALPHA * x + gt2 * f, ln2_g[l], ln2_b[l])
        if need_ctx:
            ctx = layer_norm(DEEPNORM_ALPHA * ctx + gt1c * mo_c, ln1_g[l], ln1_b[l])
            hc = ctx * (1.0 + sc2c) + sh2c
            fc = moe_ffn(hc.reshape(-1, D_MODEL), w_router[l], b_router[l], w1[l], b1[l], w2[l], b2[l]).reshape(ctx.shape)
            ctx = layer_norm(DEEPNORM_ALPHA * ctx + gt2c * fc, ln2_g[l], ln2_b[l])
    return x


def setup_inputs(seed=0):
    out = dict(first_inputs(seed))
    for name, value in second_inputs(seed + 1).items():
        if name != "x":
            out[name + "_2"] = value
    return out


def reference(
    x, ffn1_norm_pre, ffn1_norm_post, ffn1_w_gate, ffn1_w_up, ffn1_w_down, mix_norm_pre,
    mix_norm_post, w_in, rel_bias_table, conv_w, conv_b, lru_w_x, lru_b_x, lru_w_a, lru_b_a,
    lru_a_param, w_attn_branch, w_rec_branch, w_out, ffn2_norm_pre, ffn2_norm_post, ffn2_w_gate,
    ffn2_w_up, ffn2_w_down, c_2, ctx_2, c_ctx_2, ln0_g_2, ln0_b_2, w_ada_2, b_ada_2, w_in_2,
    mu_shift_2, w0_2, w2_decay_2, a0_2, a2_iclr_2, g2_gate_2, r_k_2, k_k_2, k_a_2, gn_g_2,
    gn_b_2, w_fno_2, b_fno_2, w_out_2, ln1_g_2, ln1_b_2, w_router_2, b_router_2, w1_2, b1_2,
    w2_2, b2_2, ln2_g_2, ln2_b_2,
):
    x = first_block(
        x, ffn1_norm_pre, ffn1_norm_post, ffn1_w_gate, ffn1_w_up, ffn1_w_down, mix_norm_pre,
        mix_norm_post, w_in, rel_bias_table, conv_w, conv_b, lru_w_x, lru_b_x, lru_w_a, lru_b_a,
        lru_a_param, w_attn_branch, w_rec_branch, w_out, ffn2_norm_pre, ffn2_norm_post,
        ffn2_w_gate, ffn2_w_up, ffn2_w_down,
    )
    return second_block(
        x, c_2, ctx_2, c_ctx_2, ln0_g_2, ln0_b_2, w_ada_2, b_ada_2, w_in_2, mu_shift_2, w0_2,
        w2_decay_2, a0_2, a2_iclr_2, g2_gate_2, r_k_2, k_k_2, k_a_2, gn_g_2, gn_b_2, w_fno_2,
        b_fno_2, w_out_2, ln1_g_2, ln1_b_2, w_router_2, b_router_2, w1_2, b1_2, w2_2, b2_2,
        ln2_g_2, ln2_b_2,
    )


_drawn_inputs = setup_inputs


def setup_inputs(seed=0):
    import zlib

    import numpy as np

    out = dict(_drawn_inputs(seed))
    spreads = {}
    factors = {'lru_b_x': 8.0,
     'lru_b_a': 8.0,
     'ffn2_norm_post': 3.153,
     'b_ada_2': 3.713,
     'w2_decay_2': 8.0,
     'a0_2': 3.046,
     'a2_iclr_2': 3.723,
     'r_k_2': 6.254,
     'k_k_2': 3.706,
     'k_a_2': 3.397,
     'gn_g_2': 8.0,
     'gn_b_2': 32.005,
     'b_fno_2': 26.88,
     'b_router_2': 26.603,
     'b1_2': 27.597,
     'b2_2': 8.0,
     'ln2_b_2': 2.806,
     'ln1_b_2': 2.717}
    for name, (base, spread) in spreads.items():
        noise = np.random.default_rng([zlib.crc32(name.encode()), seed]).standard_normal(out[name].shape)
        drawn = base * np.exp(spread * noise) if base else spread * noise
        out[name] = __import__('jax').numpy.asarray(drawn.astype(out[name].dtype))
    for name, factor in factors.items():
        out[name] = (out[name] * factor).astype(out[name].dtype)
    return out
```

```python
import math
from contextlib import ExitStack

import concourse.bass as bass
from concourse import mybir
import numpy as np

F32 = mybir.dt.float32
I32 = mybir.dt.int32
U32 = mybir.dt.uint32
ALU = mybir.AluOpType
ACT = mybir.ActivationFunctionType
AX = mybir.AxisListType.X

P = 128
D = 1024
KD = D // P
S = 256
TT = S // P
FF = 2816
FT = FF // P
HG = 4
NG = 3
NHD = NG * HG
DILATION = (1, 4, 16)
BAND = 128
EXT = 384
LH = 8
NEG = -1.0e30
CH = 64
HN = 64
RH = 8
RW = RH * HN
NE = 32
TOPK = 4
BS = 128
EJ = 8
RING = 8
SLOT = 3072
DECAY = math.exp(-0.5)
DEEP = 2.0 ** 0.25
LIMIT = 7.0
RMS_EPS, LN_EPS, GN_EPS = 1e-6, 1e-5, 64e-5


N_FFN1 = 0
N_WIN = N_FFN1 + FT
N_LRU = N_WIN + 23
N_ATT = N_LRU + 2
N_REC = N_ATT + 2
N_OUT = N_REC + 3
N_FFN2 = N_OUT + 3
N_ADA = N_FFN2 + 1
ADA = 16
N_IN2 = N_FFN2 + FT + ADA
N_OUT2 = N_IN2 + 8
N_MOE = N_OUT2 + 3
assert N_MOE % RING == 0


def ffn_slot(tag, j):
    return N_FFN1 + j if tag == "f1" else N_FFN2 + j + min(j, ADA)


IN2_TILES = (3, 3, 3, 3, 2, 2, 2, 2)


def shape_constants():
    f = np.float32
    i = np.arange(P)
    r, c = i[:, None], i[None, :]
    same = (r // CH) == (c // CH)
    cols = {}
    cols["ident"] = np.eye(P)
    for d in (0, 1):
        before = (r < c) if d == 0 else (r > c)
        cols[f"cum_exc{d}"] = -DECAY * (same & before)
        cols[f"cum_inc{d}"] = -DECAY * (same & (before | (r == c)))
        cols[f"cum_rem{d}"] = -DECAY * (same & ~before & (r != c))
        cols[f"pair{d}"] = np.concatenate([same & before, same & (before | (r == c))], 1)
        after = (r > c) if d == 0 else (r < c)
        cols[f"first{d}"] = after & ((r // 2) == (c // 2))
    b = 2
    while b < CH:
        cols[f"lev{b}"] = ((r // (2 * b)) == (c // (2 * b))) & ((r // b) != (c // b))
        b *= 2
    cols["lev1"] = ((r // 2) == (c // 2)) & (r != c)
    cols["chunks"] = -DECAY * ((r // CH) == np.arange(2)[None, :])
    k = np.arange(HN)
    ang = 2 * np.pi * np.outer(k, k) / HN
    z = np.zeros((HN, HN))
    blk = lambda m: np.block([[m, z], [z, m]])
    cols["dft_c"] = np.concatenate([blk(np.cos(ang)), blk(np.sin(ang))], 1) / np.sqrt(HN)
    t = np.arange(S)
    ang = 2 * np.pi * ((np.outer(t, t)) % S) / S
    for tt in range(TT):
        cols[f"dft_t{tt}"] = np.cos(ang[tt * P:(tt + 1) * P]) / np.sqrt(S)
        cols[f"dft_s{tt}"] = -np.sin(ang[tt * P:(tt + 1) * P]) / np.sqrt(S)
    cols["earlier"] = r < c
    cols["ones"] = np.ones((P, P))
    cols["slots"] = np.tile(np.arange(S)[None], (P, 1))
    names, at = {}, 0
    for n, a in cols.items():
        names[n] = (at, a.shape[1])
        at += a.shape[1]
    blob = np.concatenate([np.asarray(a, np.float64) for a in cols.values()], 1).astype(f)
    return names, blob


def bias_constants():
    buckets, far = 32, 2048
    dist = 255 - np.arange(EXT)
    half = buckets // 2
    nf = np.maximum(dist, 1).astype(np.float32)
    large = half + (np.log(nf / half) / math.log(far / half) * (buckets - half)).astype(np.int32)
    bucket = np.where(dist < half, dist, np.minimum(large, buckets - 1))
    hot = np.zeros((buckets, NG, EXT), np.float32)
    mask = np.full((1, NG, EXT), NEG, np.float32)
    for g, d in enumerate(DILATION):
        ok = (dist >= 0) & (dist % d == 0) & (dist <= BAND * d)
        hot[bucket[ok], g, np.nonzero(ok)[0]] = 1.0
        mask[0, g, ok] = 0.0
    return hot.reshape(buckets, NG * EXT), mask.reshape(1, NG * EXT)


CONST_AT, CONST_BLOB = shape_constants()
NCONST = CONST_BLOB.shape[1]
BIAS_HOT, BIAS_MASK = bias_constants()

COLUMN_ROWS = [("ffn1_norm_pre", 8), ("mix_norm_pre", 8), ("ffn2_norm_pre", 8), ("conv_w", 32),
               ("conv_b", 8), ("lru_b_x", 8), ("lru_b_a", 8), ("lru_a_param", 8), ("mu_shift_2", 16),
               ("c_2", 8), ("c_ctx_2", 8), ("b_fno_2", 4), ("b_ada_2", 48)]
ROWS_ACT = 6
COL_AT, _n = {}, 0
for _name, _rows in COLUMN_ROWS:
    if _n // P != (_n + _rows - 1) // P:
        _n = -(-_n // P) * P
    COL_AT[_name] = _n
    _n += _rows
NCOLS = _n
assert NCOLS <= 2 * P


SHARED = {
    "pe_1": (("cols_tp", 1), ("ext_mm", 12), ("qk", 16), ("v", 4), ("att_scores", 8), ("rec", 21), ("lru", 14),
             ("attb", 6), ("recb", 5), ("hT2_tp", 8), ("in2", 12), ("xcs_mm", 8), ("spec_mm", 4), ("fno_mm", 4),
             ("rw_tp", 2), ("row_mm", 4), ("h2_tp", 4), ("logits", 2), ("b1_tp", 1), ("rank_mm", 1), ("gw_tp", 1),
             ("acc_mm", 2), ("gathered", 0)),
    "pe_2": (("att_tp", 8), ("up", 0)),
    "pe_3": (("att_pv", 4), ("scat", 0)),
    "act_1": (("sp_exp", 1), ("qk_out0", 12), ("v_out0", 4), ("att_exp", 8), ("gate_out", 24), ("lru_gate", 16),
              ("lru_tanh", 8), ("lru_sqrt", 1), ("cs", 2), ("p_read", 20), ("lora", 2), ("xcs", 8), ("spec", 4),
              ("fno", 4), ("catT", 2), ("rowb", 4), ("ek", 2), ("sig", 0)),
    "act_2": (("att_pT", 8), ("xs", 0)),
    "dve_1": (("cols", 2), ("ext", 12), ("qk_out1", 12), ("v_out1", 4), ("att_scored", 8), ("decay8", 1),
              ("xr_out", 8), ("lru_gx", 8), ("lru_ratio", 1), ("att_merged", 8), ("recT", 1), ("rec_merged", 8),
              ("cmu", 3), ("modT", 2), ("hT2", 16), ("lat_shift", 16), ("b1T", 1), ("cnt", 1), ("GT", 1), ("acc0", 3),
              ("act", 0)),
    "dve_2": (("att_max", 8), ("xc", 8), ("log_a", 8), ("gw", 2), ("glu", 0)),
    "dve_3": (("att_prob", 8), ("h2", 2), ("h2T", 4), ("top", 2), ("lin", 0)),
    "dve_4": (("attnT", 4), ("mask", 2), ("sel", 0)),
    "pool_1": (("ctx_shift", 10), ("bb", 0)),
}
EVENT = {}
for _sem, _events in SHARED.items():
    _n = 0
    for _name, _times in _events:
        EVENT[_name] = (_sem, _n)
        _n += _times


def build(nc, x, out):
    with ExitStack() as ctx:
        table = {}

        counted = {}

        def sems(name):
            name = EVENT.get(name, (name, 0))[0]
            if name not in table:
                table[name] = ctx.enter_context(nc.semaphore(name))
            return table[name]

        def up(name):
            shared, base = EVENT.get(name, (name, 0))
            counted[name] = counted.get(name, 0) + 1
            if shared != name:
                counted[shared] = counted.get(shared, 0) + 1
                assert counted[shared] == base + counted[name], name
            return sems(name), 1

        def at(name, n):
            return sems(name), n + EVENT.get(name, (name, 0))[1]

        def now(name):
            return at(name, counted[name])

        def sb(name, shape, dt=F32):
            return ctx.enter_context(nc.sbuf_tensor(name, shape, dt))

        AW = 22000
        ring = sb("ring", [P, RING, SLOT])
        h = sb("h", [P, TT, D])
        const = sb("const", [P, NCONST])
        cols = sb("cols", [P, NCOLS])
        stat = sb("stat", [P, 64])
        arena = sb("arena", [P, AW])
        ps = ctx.enter_context(nc.psum_tensor("ps", [P, 8, 512], F32))
        shear = nc.dram_tensor("shear", [NHD, P, EXT], F32, kind="Internal")

        def k_(name, lo=0, n=None, rows=P):
            pos, w = CONST_AT[name]
            return const[0:rows, pos + lo:pos + lo + (w if n is None else n)]

        ident = k_("ident")

        def col(name, i=0, n=1):
            return cols[:, COL_AT[name] + i:COL_AT[name] + i + n]

        def area(base, sizes, start=0, limit=None):
            res, pos = [], start
            for shape in sizes:
                n = int(np.prod(shape[1:]))
                v = base[0:shape[0], pos:pos + n]
                if len(shape) == 3:
                    v = v.rearrange("p (a b) -> p a b", b=shape[2])
                elif len(shape) == 4:
                    v = v.rearrange("p (a b c) -> p a b c", b=shape[2], c=shape[3])
                res.append(v)
                pos += n
            assert limit is None or pos <= limit, (pos, limit)
            return res

        uT, post, hid, sil, xn, sq = area(arena, [[P, KD, S], [P, D], [P, 3, S], [P, 2, S], [P, TT, D], [P, D]], 0, AW)
        ada_sum, = area(arena, [[P, 2, 2, 384]], 7424, 9216)
        pos = 4096 + 2048 + 1280 + 1024 + 512
        bias, = area(arena, [[P, NHD, S]], AW - 3072, AW)
        hot, maskb, ext, table_sb = area(arena, [[32, NG * EXT], [P, NG * EXT], [P, NHD, EXT], [32, NHD]], pos, AW - 3072)
        rows, = area(arena, [[P, 2, P]], pos + 2 * NG * EXT + NHD * EXT + NHD, AW - 3072)
        qT, kT, v, prob, probT = area(arena, [[P, NHD, S], [P, NHD, S], [P, TT, NHD * P], [P, 2, 1152], [P, 1152]], 3072 + 1024, AW - 3072)
        attnT, = area(arena, [[P, HG, S]], 3072, 4096)
        xr, yg, gates, xc, la, lb, lt = area(
            arena, [[P, LH, S + 3], [P, LH, S], [P, 16, S], [P, LH, S], [P, LH, S], [P, LH, S], [P, LH, S]], 4096, AW)
        merged = uT
        pT, fT = area(arena, [[P, 16, 2 * S], [P, 4, S]], 0, AW)
        catT, rw, state = area(arena, [[P, 8, S], [P, TT, RW], [HN, 2, RH, HN]], 9216)
        hT2, = area(arena, [[P, KD, 2 * S]], 9216)
        ln0g, ln0b = area(arena, [[P, D], [P, D]], 9216)
        ctxt, = area(arena, [[P, TT, D]], 0)
        w2d, a2i, g2g, w0b, a0b, kkb, kab, gngb, gnbb, rkb, modT, cs, cmu, shifted = area(
            arena, [[P, RW], [P, RW], [P, 2, RW], [P, 2, RW], [P, 2, RW], [P, RW], [P, RW], [P, RW], [P, RW],
                    [P, 2, RW], [P, 48, 2], [P, 8, 2], [P, 3, 16], [P, 2, 2 * S]], 13312, AW)
        ringf = ring[:, :, :].rearrange("p a b -> p (a b)")
        (tok, sgm, av, gt, ex, kd, bb, Bp, Kp, AX_, Rt, Bt, Kt, ART, BT, KT, MbT, MkT, Ti, TiT, Zs, ME) = area(
            ringf, [[P, 8, RW], [P, RW], [P, RW], [P, RW], [P, 4, RW], [P, RW], [P, RW], [P, RW], [P, RW],
                    [P, RH, 2, HN], [P, RW], [P, RW], [P, RW], [HN, RH, 2, P], [HN, RH, P], [HN, RH, P],
                    [P, RH, 2, P], [P, RH, 2, P], [P, RH, P], [P, RH, P], [P, RH, P], [P, RH, P]], 0, RING * SLOT)
        WU, = area(ringf, [[P, RH, P]], 5632)
        QT, = area(ringf, [[HN, RH, P]], 5632 + 1024)
        FTs, = area(ringf, [[HN, 2, RH, HN]], 10752)
        yo, = area(ringf, [[P, 4, RW]], 20480)
        XCS, = area(ringf, [[P, TT, 4, 2 * P]], 16384)
        spec, = area(ringf, [[P, 4, S]], 18432)
        wbd, = area(ringf, [[P, 4, P]], 22528)
        rowb, tmpx, h2 = area(arena, [[P, 4, D], [P, TT, D], [P, TT, D]], 0, 8192)
        b1s, = area(arena, [[2 * NE, D]], 8192, 9216)
        ln1g, ln1b = area(arena, [[P, D], [P, D]], 11264, 13312)
        h2T, = area(arena, [[P, KD, S]], 9216)
        (acc, wr, brb, b2s, ln2g, ln2b, b1T, rk, gw, mask, lg, top, idxf, ek, hot32, idx, cnt) = area(
            arena, [[P, TT, D], [P, KD, NE], [P, NE], [NE, D], [P, D], [P, D], [P, 2 * EJ, NE + 1], [P, TT, NE + 1], [P, TT, NE + 1],
                    [P, TT, NE], [P, TT, NE], [P, TT, 8], [P, TT, 8], [P, TT, 8], [P, NE], [P, TT, 8], [1, NE + 1]], 13312, 20480)
        idx, cnt = idx.bitcast(U32), cnt.bitcast(I32)
        def block_buffers(pos):
            res = area(arena, [[P, TT, BS], [P, TT, BS], [P, KD, BS], [BS, S], [BS, D]], pos)
            return res, pos + 4 * BS + KD * BS + S + D
        MAIN, pos = block_buffers(0)
        assert pos <= 3 * D
        MORE, pos = block_buffers(9216)
        acts, glu, lin, sig, b1e, rke, gwe, GT = area(
            arena, [[P, 2, BS], [P, 2, BS], [P, 2, BS], [P, 2, BS], [P, 2 * EJ], [P, TT], [P, TT], [NE, S]], 4096, 6144)

        def banks(b, n=1):
            return ps[:, b:b + n, :].rearrange("p a b -> p (a b)")

        def slot(n):
            return ring[:, n % RING, :]

        def blocks(w, c0, n):
            return w[:, c0:c0 + n].rearrange("(k p) n -> p k n", p=P)

        loads = {}
        for tag, f in (("f1", "ffn1"), ("f2", "ffn2")):
            for j in range(FT):
                s = slot(ffn_slot(tag, j))
                loads[ffn_slot(tag, j)] = [
                    (s[:, 0:1024].rearrange("p (k n) -> p k n", k=KD), blocks(x[f + "_w_gate"][0], j * P, P)),
                    (s[:, 1024:2048].rearrange("p (k n) -> p k n", k=KD), blocks(x[f + "_w_up"][0], j * P, P)),
                    (s[:, 2048:3072], x[f + "_w_down"][0, j * P:(j + 1) * P, :])]

        def wide(n, w, c0, width, kt):
            s = slot(n)[:, 0:kt * width].rearrange("p (k n) -> p k n", k=kt)
            loads[n] = [(s, blocks(w, c0, width))]

        for i in range(23):
            wide(N_WIN + i, x["w_in"][0], 384 * i, min(384, 8704 - 384 * i), KD)
        for i, name in enumerate(("lru_w_x", "lru_w_a")):
            loads[N_LRU + i] = [(slot(N_LRU + i)[:, 512 * q:512 * (q + 1)].rearrange("p (k n) -> p k n", k=2),
                                 x[name][0, q].rearrange("(k p) n -> p k n", p=P)) for q in range(4)]
        wide(N_ATT, x["w_attn_branch"][0], 0, 768, 4)
        wide(N_ATT + 1, x["w_attn_branch"][0], 768, 256, 4)
        for i in range(3):
            wide(N_REC + i, x["w_rec_branch"][0], 384 * i, min(384, 1024 - 384 * i), KD)
            kt = min(3, KD - 3 * i)
            for base, name in ((N_OUT, "w_out"), (N_OUT2, "w_out_2")):
                loads[base + i] = [(slot(base + i)[:, 0:kt * D].rearrange("p (k n) -> p k n", k=kt),
                                    x[name][0, 3 * i * P:(3 * i + kt) * P, :].rearrange("(k p) n -> p k n", p=P))]
        for i in range(ADA):
            wide(N_ADA + 2 * i, x["w_ada_2"][0], 384 * i, 384, KD)
        c0 = 0
        for i, n in enumerate(IN2_TILES):
            wide(N_IN2 + i, x["w_in_2"][0], c0 * P, n * P, KD)
            c0 += n
        landed_at, per_slot = {}, [0] * RING
        for n in range(N_MOE):
            per_slot[n % RING] += 16 * len(loads[n])
            landed_at[n] = per_slot[n % RING]

        def landed(e, n):
            e.wait_ge(*at(f"w_landed{n % RING}", landed_at[n]))

        def send(e, n):
            if n == 2:
                e.wait_ge(*at("rows_in_a", 16 * ROWS_ACT))
                e.wait_ge(*at("rows_in_p", 16 * (len(COLUMN_ROWS) - ROWS_ACT)))
            if n == N_OUT2:
                e.wait_ge(*at("v_end", 4))
            if n >= RING:
                e.wait_ge(*at("w_used", n - RING + 1))
            for dst, src in loads[n]:
                e.dma_start(dst, src).then_inc(sems(f"w_landed{n % RING}"), 16)

        NORMS = ["f1", "p1", "mix", "pm", "f2", "p2"]
        PRES = ["f1", "mix", "f2"]
        FFNS = ["f1", "f2"]
        POSTS = ["p1", "pm", "p2"]

        def nth(phases, tag, per, i):
            return per * phases.index(tag) + i

        def norm_stats_act(a, tag, src, after):
            for tt in range(TT):
                a.wait_ge(*at(*after(tt)))
                a.activation(sq[:, :], src(tt), ACT.Square, scale=1.0 / 32, accum_out=stat[:, tt:tt + 1]).then_inc(*up("norm_ss"))
                a.wait_ge(*now("norm_ss"))
            a.wait_ge(*at("norm_ms", nth(NORMS, tag, 1, 1)))
            a.activation(stat[:, 4:6], stat[:, 2:4], ACT.Sqrt).then_inc(*up("norm_root"))

        def norm_stats_dve(d, tag, eps=RMS_EPS):
            d.wait_ge(*at("norm_ss", nth(NORMS, tag, TT, TT)))
            d.tensor_scalar_add(stat[:, 2:4], stat[:, 0:2], eps).then_inc(*up("norm_ms"))
            d.wait_ge(*now("norm_ms"))
            d.wait_ge(*at("norm_root", nth(NORMS, tag, 1, 1)))
            d.reciprocal(stat[:, 6:8], stat[:, 4:6]).then_inc(*up("dve_own"))
            d.wait_ge(*now("dve_own"))

        def pre_act(a, tag, prev):
            norm_stats_act(a, tag, lambda tt: h[:, tt, :], prev)

        def pre_dve(d, tag, gain):
            norm_stats_dve(d, tag)
            for tt in range(TT):
                d.tensor_scalar(xn[:, tt, :], h[:, tt, :], stat[:, 6 + tt:7 + tt], None, ALU.mult).then_inc(*up("xn"))
                d.wait_ge(*now("xn"))
            for b in range(4):
                tt, k0 = b // 2, 4 * (b % 2)
                d.wait_ge(*at("xn_tp", nth(PRES, tag, 4, b + 1)))
                d.tensor_tensor(uT[:, k0:k0 + 4, tt * P:(tt + 1) * P], ps[:, b, :].rearrange("p (a b) -> p a b", b=P),
                                         col(gain, k0, 4).unsqueeze(2).to_broadcast([P, 4, P]), ALU.mult).then_inc(*up("uT"))
                d.wait_ge(*now("uT"))

        def pre_pe(pe, tag):
            for b in range(4):
                tt, k0 = b // 2, 4 * (b % 2)
                pe.wait_ge(*at("xn", nth(PRES, tag, TT, tt + 1)))
                for k in range(4):
                    ins = pe.transpose(ps[:, b, k * P:(k + 1) * P], xn[:, tt, (k0 + k) * P:(k0 + k + 1) * P], ident)
                ins.then_inc(*up("xn_tp"))

        def ffn_up_pe(pe, tag, n, j):
            landed(pe, n)
            if j >= 2:
                pe.wait_ge(*at("ffn_hid", nth(FFNS, tag, FT, j - 1)))
            s = slot(n)
            for half in range(2):
                for k in range(KD):
                    col0 = half * 1024 + k * P
                    ins = pe.matmul(ps[:, j % 2, half * S:(half + 1) * S], s[:, col0:col0 + P], uT[:, k, :],
                                        start=(k == 0), stop=(k == KD - 1))
            ins.then_inc(*up("ffn_up"))

        def ffn_down_pe(pe, tag, n, j):
            pe.wait_ge(*at("ffn_hid", nth(FFNS, tag, FT, j + 1)))
            s = slot(n)
            for tt in range(TT):
                for nh in range(2):
                    ins = pe.matmul(ps[:, 4 + 2 * tt + nh, :], hid[:, j % 3, tt * P:(tt + 1) * P],
                                        s[:, 2048 + nh * 512:2048 + (nh + 1) * 512], start=(j == 0), stop=(j == FT - 1))
            ins.then_inc(*up("w_used"))

        def ffn_pe(pe, tag, beside):
            pre_pe(pe, tag)
            pe.wait_ge(*at("uT", nth(PRES, tag, 4, 4)))
            for j in range(FT + 1):
                if j < FT:
                    ffn_up_pe(pe, tag, ffn_slot(tag, j), j)
                if j:
                    ffn_down_pe(pe, tag, ffn_slot(tag, j - 1), j - 1)
                    beside(j - 1)

        def ffn_act(a, tag, prev):
            pre_act(a, tag, prev)
            for j in range(FT):
                a.wait_ge(*at("ffn_up", nth(FFNS, tag, FT, j + 1)))
                if j >= 2:
                    a.wait_ge(*at("ffn_hid", nth(FFNS, tag, FT, j - 1)))
                a.activation(sil[:, j % 2, :], ps[:, j % 2, 0:S], ACT.Silu).then_inc(*up("ffn_sil"))

        def ffn_dve(d, tag, gain, beside):
            pre_dve(d, tag, gain)
            for j in range(FT):
                d.wait_ge(*at("ffn_sil", nth(FFNS, tag, FT, j + 1)))
                if j >= 3:
                    d.wait_ge(*at("w_used", ffn_slot(tag, j - 3) + 1))
                d.tensor_tensor(hid[:, j % 3, :], sil[:, j % 2, :], ps[:, j % 2, S:2 * S], ALU.mult).then_inc(*up("ffn_hid"))
                beside(j)

        def post_act(a, tag, done):
            norm_stats_act(a, tag, lambda tt: banks(4 + 2 * tt, 2), lambda tt: done)

        def post_dve(d, tag, factor):
            norm_stats_dve(d, tag)
            d.wait_ge(*at("post_in", 16 * POSTS.index(tag) + 16))
            for tt in range(TT):
                d.scalar_tensor_tensor(xn[:, tt, :], banks(4 + 2 * tt, 2), stat[:, 6 + tt:7 + tt], post[:, :], ALU.mult, ALU.mult).then_inc(*up("post_free"))
                d.wait_ge(*now("post_free"))
            for tt in range(TT):
                d.scalar_tensor_tensor(h[:, tt, :], xn[:, tt, :], factor, h[:, tt, :], ALU.mult, ALU.add).then_inc(*up("post_h"))
                d.wait_ge(*now("post_h"))


        SCALE = 1.0 / math.sqrt(P)

        def proj_pe(pe, tag, n, tiles, i0, freed, kt=KD, src=None, width=S, lo=0):
            landed(pe, n)
            src = uT if src is None else src
            w = slot(n)[:, 0:kt * tiles * P].rearrange("p (k n) -> p k n", k=kt)
            for c in range(tiles):
                freed(i0 + c)
                for k in range(kt):
                    ins = pe.matmul(ps[:, (i0 + c) % 4, 0:width], w[:, k, c * P:(c + 1) * P], src[:, k, lo:lo + width],
                                        start=(k == 0), stop=(k == kt - 1))
                ins.then_inc(*up("w_used" if c == tiles - 1 else tag))

        def tiles_of(n0, widths):
            res, i, short = [], 0, 0
            for s, w in enumerate(widths):
                for c in range(w):
                    if c == w - 1:
                        res.append((n0 + s, i, "w_used", n0 + s + 1))
                    else:
                        short += 1
                        res.append((n0 + s, i, "", short))
                    i += 1
            return res

        def tile_done(e, tag, t):
            e.wait_ge(*at(t[2] or tag, t[3]))

        QK = tiles_of(N_WIN, (3,) * 8)
        REC = tiles_of(N_WIN + 12, (3,) * 10 + (2,))

        ROWS_A = COL_AT["b_fno_2"] + 4

        def setup_pe(pe):
            pe.wait_ge(*at("rows_in_a", 16 * ROWS_ACT))
            pe.wait_ge(*at("rows_in_p", 16 * (len(COLUMN_ROWS) - ROWS_ACT)))
            pe.wait_ge(*at("const_in", 16))
            pe.transpose(ps[:, 0, 0:ROWS_A], rows[0:ROWS_A, 0, :], k_("ident", 0, ROWS_A, ROWS_A))
            pe.transpose(ps[:, 0, P:P + 48], rows[0:48, 1, :], k_("ident", 0, 48, 48)).then_inc(*up("cols_tp"))

        def bias_pe(pe, i):
            if 0 <= i < NHD:
                pe.wait_ge(*at("hot_in", 48))
                if i >= 2:
                    pe.wait_ge(*at("ext", i - 1))
                pe.matmul(ps[:, 2 + i % 2, 0:EXT], table_sb[:, i:i + 1].to_broadcast([32, P]),
                                      hot[:, (i // HG) * EXT:(i // HG + 1) * EXT], start=True, stop=True).then_inc(*up("ext_mm"))

        def setup_dve(d):
            d.wait_ge(*at("cols_tp", 1))
            d.tensor_copy(cols[:, P:NCOLS], ps[:, 0, P:NCOLS]).then_inc(*up("cols"))
            d.tensor_copy(cols[:, 0:ROWS_A], ps[:, 0, 0:ROWS_A]).then_inc(*up("cols"))
            d.wait_ge(*now("cols"))

        def bias_dve(d, i):
            if 0 <= i < NHD:
                d.wait_ge(*at("hot_in", 48))
                d.wait_ge(*at("ext_mm", i + 1))
                g = i // HG
                d.tensor_tensor(ext[:, i, :], ps[:, 2 + i % 2, 0:EXT], maskb[:, g * EXT:(g + 1) * EXT], ALU.add).then_inc(*up("ext"))

        def setup_pool(p):
            for i in range(NHD):
                p.wait_ge(*at("ext", i + 1))
                p.dma_start(shear.ap()[i], ext[:, i, :]).then_inc(sems("ext_out"), 16)
            p.wait_ge(*at("ext_out", 16 * NHD))
            src = bass.AP(shear, P - 1, [[EXT - 1, P], [P * EXT, NHD], [1, S]])
            p.dma_start(bias[:, :, :], src).then_inc(sems("bias_in"), 16)

        def qkv_pe(pe):
            pre_pe(pe, "mix")
            pe.wait_ge(*at("uT", nth(PRES, "mix", 4, 4)))

            def freed(i):
                if i >= 4:
                    pe.wait_ge(*at(f"qk_out{i % 2}", (i - 4) // 2 + 1))
            for s in range(8):
                proj_pe(pe, "qk", N_WIN + s, 3, 3 * s, freed)
            for s in range(4):
                n = N_WIN + 8 + s
                landed(pe, n)
                w = slot(n)[:, 0:KD * 384].rearrange("p (k n) -> p k n", k=KD)
                for tt in range(TT):
                    i = 24 + 2 * s + tt
                    if s < 2:
                        pe.wait_ge(*at(f"qk_out{i % 2}", (i - 4) // 2 + 1))
                    else:
                        pe.wait_ge(*at(f"v_out{tt}", s - 1))
                    for k in range(KD):
                        ins = pe.matmul(ps[:, i % 4, 0:384], uT[:, k, tt * P:(tt + 1) * P], w[:, k, :],
                                            start=(k == 0), stop=(k == KD - 1))
                    ins.then_inc(*up("w_used" if tt else "v"))

        def qkv_out(e, copy, parity):
            e.wait_ge(*at("ext_out", 16 * NHD))
            for t in QK:
                if t[1] % 2 == parity:
                    tile_done(e, "qk", t)
                    dst = qT if t[1] < NHD else kT
                    copy(dst[:, t[1] % NHD, :], ps[:, t[1] % 4, 0:S]).then_inc(*up(f"qk_out{parity}"))
            for s in range(4):
                if parity:
                    e.wait_ge(*at("w_used", N_WIN + 9 + s))
                else:
                    e.wait_ge(*at("v", s + 1))
                copy(v[:, parity, 384 * s:384 * (s + 1)], ps[:, 2 * (s % 2) + parity, 0:384]).then_inc(*up(f"v_out{parity}"))

        SPAN = [(0, NG * P), (NG * P, NG * S)]

        def attn_pe(pe):
            for par in range(2):
                pe.wait_ge(*at(f"qk_out{par}", 12))
                pe.wait_ge(*at(f"v_out{par}", 4))
            for i in range(HG + 1):
                if i < HG:
                    if i:
                        pe.wait_ge(*at("att_scored", 2 * i))
                    for qt in range(TT):
                        for g in range(NG):
                            hd, nk = g * HG + i, P * (qt + 1)
                            o = banks(qt, 1 + qt)
                            ins = pe.matmul(o[:, g * nk:(g + 1) * nk], qT[:, hd, qt * P:(qt + 1) * P], kT[:, hd, 0:nk],
                                                start=True, stop=True)
                        ins.then_inc(*up("att_scores"))
                if i:
                    j = i - 1
                    for qt in range(TT):
                        pe.wait_ge(*at("att_prob", 2 * j + qt + 1))
                        if qt == 0 and j:
                            pe.wait_ge(*at("att_pT", 2 * j))
                        for b in range(3 * (qt + 1)):
                            ins = pe.transpose(banks(3 + qt, 1 + qt)[:, b * P:(b + 1) * P],
                                                   prob[:, j % 2, SPAN[qt][0] + b * P:SPAN[qt][0] + (b + 1) * P], ident)
                        ins.then_inc(*up("att_tp"))
                    if j >= 2:
                        pe.wait_ge(*at("attnT", j - 1))
                    for qt in range(TT):
                        pe.wait_ge(*at("att_pT", 2 * j + qt + 1))
                        nb = 3 * (qt + 1)
                        for b in range(nb):
                            g, kt_ = b // (qt + 1), b % (qt + 1)
                            hd = g * HG + j
                            ins = pe.matmul(ps[:, 6 + j % 2, qt * P:(qt + 1) * P], v[:, kt_, hd * P:(hd + 1) * P],
                                                probT[:, SPAN[qt][0] + b * P:SPAN[qt][0] + (b + 1) * P],
                                                start=(b == 0), stop=(b == nb - 1))
                    ins.then_inc(*up("att_pv"))

        def attn_dve(d):
            d.wait_ge(*at("bias_in", 16))
            for i in range(HG + 1):
                if i < HG:
                    for qt in range(TT):
                        lo, w = SPAN[qt]
                        p_ = prob[:, i % 2, lo:lo + w]
                        if i >= 2:
                            d.wait_ge(*at("att_tp", 2 * (i - 1)))
                        d.wait_ge(*at("att_scores", 2 * i + qt + 1))
                        bs = bias[:, i:NHD:HG, (P if qt == 0 else 0):S]
                        nk = P * (qt + 1)
                        d.scalar_tensor_tensor(p_.rearrange("p (g k) -> p g k", k=nk),
                                                        banks(qt, 1 + qt)[:, 0:w].rearrange("p (g k) -> p g k", k=nk),
                                                        SCALE, bs, ALU.mult, ALU.add).then_inc(*up("att_scored"))
                        d.wait_ge(*now("att_scored"))
                        c = 8 + 8 * (i % 2) + 4 * qt
                        d.tensor_reduce(stat[:, c:c + 1], p_, AX, ALU.max, negate=True).then_inc(*up("att_max"))
                        d.wait_ge(*now("att_max"))
                if i:
                    for qt in range(TT):
                        c = 8 + 8 * ((i - 1) % 2) + 4 * qt
                        lo, w = SPAN[qt]
                        p_ = prob[:, (i - 1) % 2, lo:lo + w]
                        d.wait_ge(*at("att_exp", 2 * (i - 1) + qt + 1))
                        d.reciprocal(stat[:, c + 2:c + 3], stat[:, c + 1:c + 2]).then_inc(*up("dve_own"))
                        d.wait_ge(*now("dve_own"))
                        d.tensor_scalar(p_, p_, stat[:, c + 2:c + 3], None, ALU.mult).then_inc(*up("att_prob"))
                    d.wait_ge(*at("att_pv", i))
                    d.tensor_copy(attnT[:, i - 1, :], ps[:, 6 + (i - 1) % 2, 0:S]).then_inc(*up("attnT"))

        def attn_act(a):
            for i in range(HG + 1):
                if i < HG:
                    for qt in range(TT):
                        c = 8 + 8 * (i % 2) + 4 * qt
                        lo, w = SPAN[qt]
                        p_ = prob[:, i % 2, lo:lo + w]
                        a.wait_ge(*at("att_max", 2 * i + qt + 1))
                        a.activation(p_, p_, ACT.Exp, bias=stat[:, c:c + 1], accum_out=stat[:, c + 1:c + 2]).then_inc(*up("att_exp"))
                        a.wait_ge(*now("att_exp"))
                if i:
                    for qt in range(TT):
                        lo, w = SPAN[qt]
                        a.wait_ge(*at("att_tp", 2 * (i - 1) + qt + 1))
                        if i >= 2 and qt == 0:
                            a.wait_ge(*at("att_pv", i - 1))
                        a.activation(probT[:, lo:lo + w], banks(3 + qt, 1 + qt)[:, 0:w], ACT.Copy).then_inc(*up("att_pT"))

        def rec_pe(pe):
            pe.wait_ge(*at("attnT", HG))

            def freed(i):
                if i >= 4:
                    if i - 4 < LH:
                        pe.wait_ge(*at("xr_out", i - 3))
                    else:
                        pe.wait_ge(*at("gate_out", i - 4 - LH + 1))
            for s in range(11):
                proj_pe(pe, "rec", N_WIN + 12 + s, 3 if s < 10 else 2, 3 * s, freed)
            pe.wait_ge(*at("xc", LH))
            for gi in range(2):
                n = N_LRU + gi
                landed(pe, n)
                w = slot(n)[:, 0:2048].rearrange("p (q k n) -> p q k n", q=4, k=2)
                for o in range(LH):
                    i = gi * LH + o
                    if i < 4:
                        pe.wait_ge(*at("gate_out", 24 - 3 + i))
                    elif i >= 8:
                        pe.wait_ge(*at("lru_gate", i - 7))
                    for k in range(2):
                        ins = pe.matmul(ps[:, i % 8, 0:S], w[:, o // 2, k, (o % 2) * P:(o % 2 + 1) * P], xc[:, o // 2 * 2 + k, :],
                                            start=(k == 0), stop=(k == 1))
                    ins.then_inc(*up("w_used" if o == LH - 1 else "lru"))
            i = 0
            for n, tiles in ((N_ATT, 6), (N_ATT + 1, 2)):
                def freed(i):
                    if i < 4:
                        pe.wait_ge(*at("lru_gate", 8 + i + 1))
                    else:
                        pe.wait_ge(*at("att_merged", i - 3))
                proj_pe(pe, "attb", n, tiles, i, freed, kt=4, src=attnT)
                i += tiles
            pe.wait_ge(*at("recT", 1))
            i = 0
            for n, tiles in ((N_REC, 3), (N_REC + 1, 3), (N_REC + 2, 2)):
                def freed(i):
                    if i < 4:
                        pe.wait_ge(*at("att_merged", i + 5))
                    else:
                        pe.wait_ge(*at("rec_merged", i - 3))
                proj_pe(pe, "recb", n, tiles, i, freed, src=lb)
                i += tiles
            pe.wait_ge(*at("rec_merged", LH))
            out_pe(pe, N_OUT, merged)

        def out_pe(pe, n0, src):
            for k in range(KD):
                n = n0 + k // 3
                if k % 3 == 0:
                    landed(pe, n)
                w = slot(n)[:, (k % 3) * D:(k % 3 + 1) * D]
                for tt in range(TT):
                    for nh in range(2):
                        ins = pe.matmul(ps[:, 4 + 2 * tt + nh, :], src[:, k, tt * P:(tt + 1) * P], w[:, nh * 512:(nh + 1) * 512],
                                            start=(k == 0), stop=(k == KD - 1))
                if k % 3 == 2 or k == KD - 1:
                    ins.then_inc(*up("w_used"))

        ATTB = tiles_of(N_ATT, (6, 2))
        RECB = tiles_of(N_REC, (3, 3, 2))
        LRU_G = tiles_of(N_LRU, (LH, LH))

        def rec_dve(d):
            z, y, y2, acc, m8 = (stat[:, 24 + 8 * i:32 + 8 * i] for i in range(5))
            d.wait_ge(*at("sp_exp", 1))
            d.tensor_scalar_add(y, z, 2.0).then_inc(*up("dve_own"))
            d.wait_ge(*now("dve_own"))
            d.reciprocal(y, y).then_inc(*up("dve_own"))
            d.wait_ge(*now("dve_own"))
            d.tensor_tensor(y, y, z, ALU.mult).then_inc(*up("dve_own"))
            d.wait_ge(*now("dve_own"))
            d.tensor_tensor(y2, y, y, ALU.mult).then_inc(*up("dve_own"))
            d.wait_ge(*now("dve_own"))
            d.memset(acc, 1.0 / 19).then_inc(*up("dve_own"))
            d.wait_ge(*now("dve_own"))
            for c in (17, 15, 13, 11, 9, 7, 5, 3, 1):
                d.tensor_tensor(acc, acc, y2, ALU.mult).then_inc(*up("dve_own"))
                d.wait_ge(*now("dve_own"))
                d.tensor_scalar_add(acc, acc, 1.0 / c).then_inc(*up("dve_own"))
                d.wait_ge(*now("dve_own"))
            d.tensor_tensor(acc, acc, y, ALU.mult).then_inc(*up("dve_own"))
            d.wait_ge(*now("dve_own"))
            d.tensor_scalar(m8, col("lru_a_param", 0, 8), -1.0, 0.0, ALU.mult, ALU.max).then_inc(*up("dve_own"))
            d.wait_ge(*now("dve_own"))
            d.scalar_tensor_tensor(acc, acc, 2.0, m8, ALU.mult, ALU.add).then_inc(*up("dve_own"))
            d.wait_ge(*now("dve_own"))
            d.tensor_scalar_mul(acc, acc, -8.0).then_inc(*up("decay8"))
            d.wait_ge(*now("decay8"))
            d.memset(xr[:, :, 0:3], 0.0).then_inc(*up("dve_own"))
            d.wait_ge(*now("dve_own"))
            for t in REC[:LH]:
                j = t[1]
                tile_done(d, "rec", t)
                d.tensor_copy(xr[:, j, 3:3 + S], ps[:, j % 4, 0:S]).then_inc(*up("xr_out"))
                d.wait_ge(*now("xr_out"))
                cw = [col("conv_w", 8 * i + j) for i in range(4)]
                d.tensor_scalar(xc[:, j, :], xr[:, j, 0:S], cw[0], col("conv_b", j), ALU.mult, ALU.add).then_inc(*up("dve_own"))
                d.wait_ge(*now("dve_own"))
                for i in (1, 2):
                    d.scalar_tensor_tensor(xc[:, j, :], xr[:, j, i:i + S], cw[i], xc[:, j, :], ALU.mult, ALU.add).then_inc(*up("dve_own"))
                    d.wait_ge(*now("dve_own"))
                d.scalar_tensor_tensor(xc[:, j, :], xr[:, j, 3:3 + S], cw[3], xc[:, j, :], ALU.mult, ALU.add).then_inc(*up("xc"))
                d.wait_ge(*now("xc"))
            for t in LRU_G:
                if t[1] < LH:
                    d.wait_ge(*at("lru_gate", t[1] + 1))
                    d.tensor_tensor(lt[:, t[1], :], lb[:, t[1], :], xc[:, t[1], :], ALU.mult).then_inc(*up("lru_gx"))
                    d.wait_ge(*now("lru_gx"))
                else:
                    j = t[1] - LH
                    d.wait_ge(*at("lru_gate", t[1] + 1))
                    d.tensor_scalar(la[:, j, :], la[:, j, :], acc[:, j:j + 1], None, ALU.mult).then_inc(*up("log_a"))
                    d.wait_ge(*now("log_a"))
            d.wait_ge(*at("lru_tanh", LH))
            d.tensor_scalar_add(xc[:, :, :], lb[:, :, :], 1.0).then_inc(*up("dve_own"))
            d.wait_ge(*now("dve_own"))
            d.reciprocal(xc[:, :, :], xc[:, :, :]).then_inc(*up("dve_own"))
            d.wait_ge(*now("dve_own"))
            d.tensor_tensor(xc[:, :, :], xc[:, :, :], lb[:, :, :], ALU.mult).then_inc(*up("lru_ratio"))
            d.wait_ge(*now("lru_ratio"))
            for t in ATTB:
                tile_done(d, "attb", t)
                d.tensor_tensor(merged[:, t[1], :], ps[:, t[1] % 4, 0:S], gates[:, t[1], :], ALU.mult).then_inc(*up("att_merged"))
                d.wait_ge(*now("att_merged"))
            d.wait_ge(*at("lru_sqrt", 1))
            d.tensor_tensor(lt[:, :, :], lt[:, :, :], xc[:, :, :], ALU.mult).then_inc(*up("dve_own"))
            d.wait_ge(*now("dve_own"))
            for j in range(LH):
                d.tensor_tensor_scan(lb[:, j, :], la[:, j, :], lt[:, j, :], 0.0, ALU.mult, ALU.add).then_inc(*up("dve_own"))
                d.wait_ge(*now("dve_own"))
            d.tensor_tensor(lb[:, :, :], lb[:, :, :], yg[:, :, :], ALU.mult).then_inc(*up("recT"))
            d.wait_ge(*now("recT"))
            for t in RECB:
                tile_done(d, "recb", t)
                d.tensor_tensor(gates[:, 8 + t[1], :], ps[:, t[1] % 4, 0:S], gates[:, 8 + t[1], :], ALU.mult).then_inc(*up("dve_own"))
                d.wait_ge(*now("dve_own"))
                d.tensor_tensor(merged[:, t[1], :], merged[:, t[1], :], gates[:, 8 + t[1], :], ALU.add).then_inc(*up("rec_merged"))
                d.wait_ge(*now("rec_merged"))

        def softplus_act(a):
            z = stat[:, 24:32]
            a.activation(z, col("lru_a_param", 0, 8), ACT.Abs).then_inc(*up("act_own"))
            a.wait_ge(*now("act_own"))
            a.activation(z, z, ACT.Exp, scale=-1.0).then_inc(*up("sp_exp"))
            a.wait_ge(*now("sp_exp"))

        def rec_act(a):
            for t in REC[LH:]:
                j = t[1] - LH
                if j == 0:
                    a.wait_ge(*at("attnT", HG))
                tile_done(a, "rec", t)
                if j < LH:
                    a.activation(yg[:, j, :], ps[:, t[1] % 4, 0:S], ACT.Gelu_apprx_tanh).then_inc(*up("gate_out"))
                else:
                    a.activation(gates[:, j - LH, :], ps[:, t[1] % 4, 0:S], ACT.Sigmoid).then_inc(*up("gate_out"))
            for t in LRU_G:
                tile_done(a, "lru", t)
                dst = lb if t[1] < LH else la
                a.activation(dst[:, t[1] % LH, :], ps[:, t[1] % 8, 0:S], ACT.Sigmoid,
                                        bias=col("lru_b_x" if t[1] < LH else "lru_b_a", t[1] % LH)).then_inc(*up("lru_gate"))
            for j in range(LH):
                a.wait_ge(*at("log_a", j + 1))
                a.wait_ge(*at("lru_gx", j + 1))
                a.activation(lb[:, j, :], la[:, j, :], ACT.Tanh, scale=-1.0).then_inc(*up("lru_tanh"))
            a.wait_ge(*at("lru_tanh", LH))
            a.activation(la[:, :, :], la[:, :, :], ACT.Exp).then_inc(*up("act_own"))
            a.wait_ge(*now("act_own"))
            a.wait_ge(*at("lru_ratio", 1))
            a.activation(xc[:, :, :], xc[:, :, :], ACT.Sqrt, scale=2.0).then_inc(*up("lru_sqrt"))

        def ln_dve(d, nth_ln, src, dst, gain, shift, s0=32):
            n = len(src)
            mv, rs = stat[:, s0:s0 + 2 * n], stat[:, s0 + 2 * n:s0 + 3 * n]
            part = stat[:, s0 + 3 * n:s0 + 3 * n + 12]
            for i in range(n):
                for half in range(2):
                    d.bn_stats(part[:, 6 * half:6 * half + 6], src[i][:, half * 512:(half + 1) * 512]).then_inc(*up("dve_own"))
                    d.wait_ge(*now("dve_own"))
                d.bn_aggr(mv[:, 2 * i:2 * i + 2], part).then_inc(*up("dve_own"))
                d.wait_ge(*now("dve_own"))
            d.tensor_scalar_add(rs, mv[:, 1:2 * n:2], LN_EPS).then_inc(*up("ln_var"))
            d.wait_ge(*now("ln_var"))
            d.wait_ge(*at("ln_root", nth_ln))
            d.reciprocal(rs, rs).then_inc(*up("dve_own"))
            d.wait_ge(*now("dve_own"))
            for i in range(n):
                d.tensor_scalar(dst[i], src[i], mv[:, 2 * i:2 * i + 1], rs[:, i:i + 1], ALU.subtract, ALU.mult).then_inc(*up("dve_own"))
                d.wait_ge(*now("dve_own"))
                d.tensor_tensor(dst[i], dst[i], gain, ALU.mult).then_inc(*up("dve_own"))
                d.wait_ge(*now("dve_own"))
                d.tensor_tensor(dst[i], dst[i], shift, ALU.add).then_inc(*up("ln_x"))
                d.wait_ge(*now("ln_x"))

        def ln_act(a, nth_ln, n, s0=32):
            rs = stat[:, s0 + 2 * n:s0 + 3 * n]
            a.wait_ge(*at("ln_var", nth_ln))
            a.activation(rs, rs, ACT.Sqrt).then_inc(*up("ln_root"))

        def load2_pool(p):
            e = p

            def get(dst, src, name="in2_const"):
                e.dma_start(dst, src).then_inc(sems(name), 16)
            p.wait_ge(*at("post_free", nth(POSTS, "pm", 2, 2)))
            get(ln0g, x["ln0_g_2"].partition_broadcast(P), "ln0_in")
            get(ln0b, x["ln0_b_2"].partition_broadcast(P), "ln0_in")
            get(w2d, x["w2_decay_2"][0].rearrange("d r c -> (d r) c"))
            get(a2i, x["a2_iclr_2"][0].rearrange("d r c -> (d r) c"))
            get(g2g, x["g2_gate_2"][0].rearrange("d r c -> r d c"))
            for dst, name in ((w0b, "w0_2"), (a0b, "a0_2")):
                get(dst.rearrange("p d c -> p (d c)"), x[name][0].rearrange("d c -> (d c)").partition_broadcast(P))
            for dst, name in ((kkb, "k_k_2"), (kab, "k_a_2"), (gngb, "gn_g_2"), (gnbb, "gn_b_2")):
                get(dst, x[name][0].partition_broadcast(P))
            get(rkb.rearrange("p d c -> p (d c)"), x["r_k_2"][0].rearrange("d h n -> (d h n)").partition_broadcast(P))
            p.wait_ge(*at("ffn_up", nth(FFNS, "f2", FT, FT)))
            get(ctxt, x["ctx_2"][0].rearrange("(t p) n -> p t n", p=P), "ln0_in")
        IN2_CONST = 10 * 16

        def ada_both(i):
            return (0, 1) if i < 6 else (0,)

        def ada_dve(d, i):
            if i >= ADA:
                return
            n = N_ADA + 2 * i
            landed(d, n)
            d.wait_ge(*at("cs", 2))
            if i >= 2:
                d.wait_ge(*at("w_used", n - 3))
            w = slot(n).rearrange("p (k n) -> p k n", k=KD)
            for k in range(KD):
                for m in ada_both(i):
                    o = ada_sum[:, i % 2, m, :]
                    if k == 0:
                        d.tensor_scalar(o, w[:, 0, :], cs[:, 0, m:m + 1], None, ALU.mult).then_inc(*up(f"ada_sum{m}"))
                    else:
                        d.wait_ge(*now(f"ada_sum{m}"))
                        d.scalar_tensor_tensor(o, w[:, k, :], cs[:, k, m:m + 1], o, ALU.mult, ALU.add).then_inc(*up(f"ada_sum{m}"))

        def ada_pe(pe, i):
            if i >= ADA:
                return
            pe.wait_ge(*at("ada_sum0", KD * (i + 1)))
            if len(ada_both(i)) == 2:
                pe.wait_ge(*at("ada_sum1", KD * (i + 1)))
            for c in range(3):
                t = 3 * i + c
                for m in ada_both(i):
                    ins = pe.matmul(ps[:, 2, 2 * t + m:2 * t + m + 1], ada_sum[:, i % 2, m, c * P:(c + 1) * P], k_("ones", 0, 1), start=True, stop=True)
            ins.then_inc(*up("w_used"))

        def in2_pe(pe):
            for q in range(8):
                which, tt, kh = q // 4, (q // 2) % 2, q % 2
                pe.wait_ge(*at("ln_x", 2 * which + tt + 1))
                if q >= 4:
                    pe.wait_ge(*at("hT2", 2 * (q - 3)))
                src = ctxt if which == 0 else h
                for k in range(4):
                    kk_ = 4 * kh + k
                    ins = pe.transpose(ps[:, 4 + q % 4, k * P:(k + 1) * P], src[:, tt, kk_ * P:(kk_ + 1) * P], ident)
                ins.then_inc(*up("hT2_tp"))
            pe.wait_ge(*at("hT2", 16))

            i = 0
            for s, tiles in enumerate(IN2_TILES):
                n = N_IN2 + s
                landed(pe, n)
                w = slot(n)[:, 0:KD * tiles * P].rearrange("p (k n) -> p k n", k=KD)
                for c in range(tiles):
                    lo = 0 if both(i) else S
                    if i >= 4:
                        pe.wait_ge(*at("p_read", i - 3))
                    for k in range(KD):
                        ins = pe.matmul(ps[:, i % 4, lo:2 * S], w[:, k, c * P:(c + 1) * P], hT2[:, k, lo:2 * S],
                                            start=(k == 0), stop=(k == KD - 1))
                    ins.then_inc(*up("w_used" if c == tiles - 1 else "in2"))
                    i += 1

        def both(i):
            return 4 <= i < 14
        IN2 = tiles_of(N_IN2, IN2_TILES)

        def in2_act(a):
            a.wait_ge(*at("cols", 2))
            a.wait_ge(*at("post_free", nth(POSTS, "pm", 2, 2)))
            a.activation(cs[:, :, 0], col("c_2", 0, 8), ACT.Silu).then_inc(*up("cs"))
            a.activation(cs[:, :, 1], col("c_ctx_2", 0, 8), ACT.Silu).then_inc(*up("cs"))

        def in2_shift_act(a):
            a.wait_ge(*at("cmu", 3))
            for t in IN2:
                i = t[1]
                tile_done(a, "in2", t)
                if i >= 16:
                    a.activation(fT[:, i - 16, :], ps[:, i % 4, S:2 * S], ACT.Copy).then_inc(*up("p_read"))
                    continue
                if i == 0:
                    a.wait_ge(*at("hT2", 16))
                lo = 0 if both(i) else S
                if i >= 2:
                    a.wait_ge(*at("lat_shift", i - 1))
                    if i - 2 >= 4:
                        a.wait_ge(*at("ctx_shift", min(i - 2, 13) - 4 + 1))
                a.activation(pT[:, i, lo:2 * S], ps[:, i % 4, lo:2 * S], ACT.Copy, scale=cmu[:, 0, i:i + 1])
                if both(i):
                    a.activation(shifted[:, i % 2, 0:S], ps[:, i % 4, 0:S], ACT.Copy, scale=cmu[:, 2, i:i + 1])
                a.activation(shifted[:, i % 2, S:2 * S], ps[:, i % 4, S:2 * S], ACT.Copy, scale=cmu[:, 1, i:i + 1]).then_inc(*up("p_read"))
            a.wait_ge(*at("lat_shift", 16))
            a.wait_ge(*at("ctx_shift", 10))
            a.activation(pT[:, 12, :], pT[:, 12, :], ACT.Tanh).then_inc(*up("lora"))
            a.activation(pT[:, 14:16, S:2 * S], pT[:, 14:16, S:2 * S], ACT.Sigmoid).then_inc(*up("lora"))

        def in2_dve(d):
            d.wait_ge(*at("ln0_in", 48))
            ln_dve(d, 1, [ctxt[:, 0, :], ctxt[:, 1, :], h[:, 0, :], h[:, 1, :]],
                   [ctxt[:, 0, :], ctxt[:, 1, :], h[:, 0, :], h[:, 1, :]], ln0g, ln0b)
            for i, (m, s_) in enumerate(((-1.0, 1.0), (0.25, 0.0), (0.5, 0.0))):
                d.tensor_scalar(cmu[:, i, :], col("mu_shift_2", 0, 16), m, s_, ALU.mult, ALU.add).then_inc(*up("cmu"))
                d.wait_ge(*now("cmu"))
            d.wait_ge(*at("w_used", N_IN2))
            for m, n in ((0, 48), (1, 16)):
                d.tensor_tensor(modT[:, 0:n, m], ps[:, 2, 0:2 * n].rearrange("p (a b) -> p a b", b=2)[:, :, m],
                                col("b_ada_2", 0, n), ALU.add).then_inc(*up("dve_own"))
                d.wait_ge(*now("dve_own"))
            for t, m in ((8, 2), (32, 1)):
                d.tensor_scalar_add(modT[:, t:t + 8, 0:m], modT[:, t:t + 8, 0:m], 1.0).then_inc(*up("modT"))
                d.wait_ge(*now("modT"))
            for q in range(8):
                which, tt, kh = q // 4, (q // 2) % 2, q % 2
                m = 1 - which
                dst = hT2[:, 4 * kh:4 * kh + 4, which * S + tt * P:which * S + (tt + 1) * P]
                d.wait_ge(*at("hT2_tp", q + 1))
                sc = modT[:, 8 + 4 * kh:12 + 4 * kh, m:m + 1].to_broadcast([P, 4, P])
                sh = modT[:, 4 * kh:4 * kh + 4, m:m + 1].to_broadcast([P, 4, P])
                d.tensor_tensor(dst, ps[:, 4 + q % 4, :].rearrange("p (a b) -> p a b", b=P), sc, ALU.mult).then_inc(*up("hT2"))
                d.wait_ge(*now("hT2"))
                d.tensor_tensor(dst, dst, sh, ALU.add).then_inc(*up("hT2"))
                d.wait_ge(*now("hT2"))
            GW = 64
            for t in IN2[:16]:
                i = t[1]
                d.wait_ge(*at("p_read", i + 1))
                o, s_ = pT[:, i, S:2 * S], shifted[:, i % 2, S:2 * S]
                og, sg_ = (z.rearrange("p (r c) -> p r c", c=GW) for z in (o, s_))
                for dst, src in ((o[:, GW:S], s_[:, 0:S - GW]), (o[:, 0:S - GW], s_[:, GW:S]),
                                 (og[:, :, 1:GW], sg_[:, :, 0:GW - 1])):
                    d.tensor_tensor(dst, dst, src, ALU.add).then_inc(*up("dve_own"))
                    d.wait_ge(*now("dve_own"))
                d.tensor_tensor(og[:, :, 0:GW - 1], og[:, :, 0:GW - 1], sg_[:, :, 1:GW], ALU.add).then_inc(*up("lat_shift"))
                d.wait_ge(*now("lat_shift"))

        def in2_pool(p):
            for i in range(4, 14):
                p.wait_ge(*at("p_read", i + 1))
                o, s_ = pT[:, i, 0:S], shifted[:, i % 2, 0:S]
                p.tensor_tensor(o[:, 1:S], o[:, 1:S], s_[:, 0:S - 1], ALU.add).then_inc(*up("pool_own"))
                p.wait_ge(*now("pool_own"))
                p.tensor_tensor(o[:, 0:S - 1], o[:, 0:S - 1], s_[:, 1:S], ALU.add).then_inc(*up("ctx_shift"))
                p.wait_ge(*now("ctx_shift"))
            p.wait_ge(*at("w_used", N_IN2 + 8))
            p.memset(wbd[:, :, :], 0.0).then_inc(*up("pool_own"))
            p.wait_ge(*now("pool_own"))
            wf = x["w_fno_2"][0].rearrange("(a b) c e -> b c a e", b=2)
            for b in range(2):
                p.dma_start(wbd[b * HN:(b + 1) * HN, :, b * HN:(b + 1) * HN], wf[b]).then_inc(sems("wbd_in"), 16)

        def fourier_pe(pe):
            pe.wait_ge(*at("p_read", 20))
            for i in range(8):
                tt, f = i // 4, i % 4
                if i >= 4:
                    pe.wait_ge(*at("xcs", i - 3))
                pe.matmul(ps[:, i % 4, 0:2 * P], fT[:, f, tt * P:(tt + 1) * P], k_("dft_c"), start=True, stop=True).then_inc(*up("xcs_mm"))
            pe.wait_ge(*at("xcs", 8))
            for f in range(4):
                for tt in range(TT):
                    for part, name in ((0, f"dft_t{tt}"), (1, f"dft_s{tt}")):
                        ins = pe.matmul(ps[:, 4 + f, 0:S], XCS[:, tt, f, part * P:(part + 1) * P], k_(name),
                                            start=(tt == 0 and part == 0), stop=(tt == 1 and part == 1))
                ins.then_inc(*up("spec_mm"))
            pe.wait_ge(*at("wbd_in", 32))
            for f in range(4):
                pe.wait_ge(*at("spec", f + 1))
                pe.matmul(ps[:, f, 0:S], wbd[:, f, :], spec[:, f, :], start=True, stop=True).then_inc(*up("fno_mm"))

        def fourier_act(a):
            for i in range(8):
                a.wait_ge(*at("xcs_mm", i + 1))
                a.activation(XCS[:, i // 4, i % 4, :], ps[:, i % 4, 0:2 * P], ACT.Copy).then_inc(*up("xcs"))
            for f in range(4):
                a.wait_ge(*at("spec_mm", f + 1))
                a.activation(spec[:, f, :], ps[:, 4 + f, 0:S], ACT.Copy).then_inc(*up("spec"))
            for f in range(4):
                a.wait_ge(*at("fno_mm", f + 1))
                a.activation(catT[:, 4 + f, :], ps[:, f, 0:S], ACT.Identity, bias=col("b_fno_2", f)).then_inc(*up("fno"))

        VISITS = []
        for section in range(2):
            for step in range(2):
                for dr in range(2):
                    VISITS.append((section, dr, step if dr == 0 else 1 - step))
        LEVELS = (2, 4, 8, 16, 32)
        NL = len(LEVELS)
        pe_w = RH * HN
        pcs = stat[0:HN, 0:16].rearrange("p (h c) -> p h c", c=2)

        def nth_row(vi, name):
            return 3 * vi + max(vi - 4, 0) + "ABKR".index(name) + 1

        def nth_col(vi, name):
            return 2 * vi + "AK".index(name) + 1 if name in "AK" else vi + max(vi - 4, 0) + "BR".index(name) + 1

        def tokv(tl, what):
            return tok[:, 4 * tl + what, :]

        def heads(ap):
            return ap.rearrange("p (h n) -> p h n", n=HN)

        def section_pe(pe, sec):
            if sec:
                pe.wait_ge(*at("S", 1 + 2 * 4))
            for tl in range(2):
                c0 = sec * S + tl * P
                for what, t0 in ((1, 4), (2, 8)) + (((0, 0),) if sec else ()):
                    if tl:
                        pe.wait_ge(*at(f"tok{what}", sec * 2 + 1 if what else 1))
                    for t in range(4):
                        ins = pe.transpose(ps[:, 1 + what, t * P:(t + 1) * P], pT[:, t0 + t, c0:c0 + P], ident)
                    ins.then_inc(*up(f"tok_tp{what}"))
            for what in (0, 1, 2) if sec else (1, 2):
                pe.wait_ge(*at(f"tok{what}", sec * 2 + 2 if what else 2))

        def section_act(a, sec):
            for tl in range(2):
                a.wait_ge(*at("tok_tp2", sec * 2 + tl + 1))
                a.activation(tokv(tl, 2), ps[:, 3, :], ACT.Copy).then_inc(*up("tok2"))
                if sec:
                    a.wait_ge(*at("tok_tp0", tl + 1))
                    a.activation(tokv(tl, 0), ps[:, 1, :], ACT.Copy).then_inc(*up("tok0"))
                a.wait_ge(*at("kk_ss", sec * 2 + tl + 1))
                a.activation(stat[:, 40:48], stat[:, 32:40], ACT.Sqrt).then_inc(*up("kk_root"))

        def section_dve(d, sec):
            for tl in range(2):
                k, kk = tokv(tl, 1), tokv(tl, 3)
                sqr = yo[:, 0, :]
                d.wait_ge(*at("tok_tp1", sec * 2 + tl + 1))
                d.tensor_copy(k, ps[:, 2, :]).then_inc(*up("tok1"))
                d.wait_ge(*now("tok1"))
                d.tensor_tensor(kk, k, kkb, ALU.mult).then_inc(*up("dve_own"))
                d.wait_ge(*now("dve_own"))
                d.tensor_tensor(sqr, kk, kk, ALU.mult).then_inc(*up("dve_own"))
                d.wait_ge(*now("dve_own"))
                d.tensor_reduce(stat[:, 32:40], heads(sqr), AX, ALU.add).then_inc(*up("kk_ss"))
                d.wait_ge(*now("kk_ss"))
                d.wait_ge(*at("kk_root", sec * 2 + tl + 1))
                d.tensor_scalar_max(stat[:, 40:48], stat[:, 40:48], 1e-12).then_inc(*up("dve_own"))
                d.wait_ge(*now("dve_own"))
                d.reciprocal(stat[:, 40:48], stat[:, 40:48]).then_inc(*up("dve_own"))
                d.wait_ge(*now("dve_own"))
                d.tensor_tensor(heads(kk), heads(kk), stat[:, 40:48].unsqueeze(2).to_broadcast([P, RH, HN]), ALU.mult).then_inc(*up("kk"))
                d.wait_ge(*now("kk"))

        def visit_pe(pe, vi):
            sec, dr, tl = VISITS[vi]
            lat = sec == 1
            nv = vi - 4
            c0 = sec * S + tl * P
            mm, tr = pe.matmul, pe.transpose
            if vi:
                pe.wait_ge(*at("S", 2 * vi + 1))
            if nv > 0:
                pe.wait_ge(*at("v_end", nv))
            dl = slice(dr * HN, (dr + 1) * HN)
            mm(ps[:, 0, :], pT[dl, 12, c0:c0 + P], w2d[dl, :], start=True, stop=True).then_inc(*up("wl"))
            mm(ps[:, 1, :], pT[dl, 13, c0:c0 + P], a2i[dl, :], start=True, stop=True).then_inc(*up("al"))
            if lat:
                mm(ps[:, 2, :], pT[:, 14 + dr, c0:c0 + P], g2g[:, dr, :], start=True, stop=True).then_inc(*up("gl"))
            pe.wait_ge(*at("sg", vi + 1))
            for b, name in ((3, "exc"), (4, "inc"), (5, "rem")):
                mm(ps[:, b, :], k_(f"cum_{name}{dr}"), sgm, start=True, stop=True)
            for hh in range(RH):
                ins = mm(ps[0:HN, 6, 2 * hh:2 * hh + 2], sgm[:, hh * HN:(hh + 1) * HN], k_("chunks"), start=True, stop=True)
            ins.then_inc(*up("cums"))
            pe.wait_ge(*at("ex", vi + 1))
            if lat:
                pe.wait_ge(*at("gate", nv + 1))
            for name, b, get in (("A", 0, lambda q: AX_[:, q, 0, :]), ("B", 4, lambda q: Bt[:, q * HN:(q + 1) * HN]),
                                 ("K", 6, lambda q: Kt[:, q * HN:(q + 1) * HN]), ("R", 2, lambda q: Rt[:, q * HN:(q + 1) * HN])):
                if name == "R" and not lat:
                    continue
                pe.wait_ge(*at("row", nth_row(vi, name)))
                for q in range(RH):
                    ins = tr(banks(b, 2)[0:HN, q * P:(q + 1) * P], get(q), ident)
                ins.then_inc(*up("row_tp"))
            pe.wait_ge(*at("col_ak", nth_col(vi, "K")))
            pe.wait_ge(*at("col_br", nth_col(vi, "R" if lat else "B")))
            wd = 2 if lat else 1
            for hg in range(2):
                mb, mk = ((2, 4), (6, 2))[hg]
                if hg:
                    pe.wait_ge(*at("Mb", 2 * vi + 1))
                for q in range(4):
                    hh = 4 * hg + q
                    mm(ps[:, hg, q * P:(q + 1) * P], ART[:, hh, 0, :], BT[:, hh, :], start=True, stop=True)
                    o = banks(mb, 2)[:, q * wd * P:(q + 1) * wd * P]
                    ins = mm(o, BT[:, hh, :], ART[:, hh, 0:wd, :], start=True, stop=True)
                ins.then_inc(*up("Mb_mm"))
                for q in range(4):
                    hh = 4 * hg + q
                    o = banks(mk, 2)[:, q * wd * P:(q + 1) * wd * P]
                    ins = mm(o, KT[:, hh, :], ART[:, hh, 0:wd, :], start=True, stop=True)
                ins.then_inc(*up("Mk_mm"))
            pe.wait_ge(*at("Mk", 2 * vi + 2))
            pe.wait_ge(*at("Ti", 2 * (NL * vi) + 1))
            for hh in range(RH):
                ins = mm(ps[:, 0, hh * HN:(hh + 1) * HN], MkT[:, hh, 0, :], tokv(tl, 2)[:, hh * HN:(hh + 1) * HN], start=True, stop=True)
            ins.then_inc(*up("X_mm"))
            for l in range(NL):
                last = l == NL - 1
                pe.wait_ge(*at("ME", NL * vi + l + 1))
                for hg in range(2):
                    pe.wait_ge(*at("Ti", 2 * (NL * vi + l) + hg + 1))
                    for q in range(4):
                        hh = 4 * hg + q
                        ins = mm(ps[:, 2 + hg, q * P:(q + 1) * P], ME[:, hh, :], Ti[:, hh, :], start=True, stop=True)
                    ins.then_inc(*up("Z_mm"))
                for hg in range(2):
                    pe.wait_ge(*at("Z", 2 * (NL * vi + l) + hg + 1))
                    for q in range(4):
                        hh = 4 * hg + q
                        if not last:
                            mm(ps[:, 4 + hg, q * P:(q + 1) * P], TiT[:, hh, :], Zs[:, hh, :], start=True, stop=True)
                        ins = mm(ps[:, 6 + hg, q * P:(q + 1) * P], Zs[:, hh, :], TiT[:, hh, :], start=True, stop=True)
                    ins.then_inc(*up("T_mm"))
            pe.wait_ge(*at("X", vi + 1))
            for hg in range(2):
                pe.wait_ge(*at("TiT", 2 * (vi) + hg + 1))
                for q in range(4):
                    hh = 4 * hg + q
                    ins = mm(ps[:, hg, q * P:(q + 1) * P], TiT[:, hh, :], AX_[:, hh, :, :], start=True, stop=True)
            ins.then_inc(*up("WU_mm"))
            pe.wait_ge(*at("WU", vi + 1))
            V = tokv(tl, 2)
            hs = [slice(q * HN, (q + 1) * HN) for q in range(RH)]
            if lat:
                for hh in range(RH):
                    ins = mm(banks(2, 2)[0:HN, hh * P:(hh + 1) * P], WU[:, hh, 0:HN], MbT[:, hh, 1, :], start=True, stop=True)
                ins.then_inc(*up("Q_mm"))
                for hh in range(RH):
                    mm(ps[:, 0, hs[hh]], MbT[:, hh, 1, :], WU[:, hh, HN:2 * HN], start=(hh == 0), stop=False, skip_group_check=True)
                    mm(ps[:, 0, hs[hh]], MkT[:, hh, 1, :], V[:, hs[hh]], start=False, stop=False, skip_group_check=True)
            for c in range(2):
                rows_ = slice(c * CH, (c + 1) * CH)
                for hh in range(RH):
                    ins = mm(ps[0:HN, 4 + c, hs[hh]], WU[rows_, hh, 0:HN], Bp[rows_, hs[hh]], start=True, stop=True)
                ins.then_inc(*up("F_mm"))
                for hh in range(RH):
                    mm(ps[0:HN, 6 + c, hs[hh]], Bp[rows_, hs[hh]], WU[rows_, hh, HN:2 * HN], start=(hh == 0), stop=False, skip_group_check=True)
                    ins = mm(ps[0:HN, 6 + c, hs[hh]], Kp[rows_, hs[hh]], V[rows_, hs[hh]], start=False, stop=False, skip_group_check=True)
                ins.then_inc(*up("G_mm"))
            if lat:
                pe.wait_ge(*at("QT", nv + 1))
            for i, c in enumerate((0, 1) if dr == 0 else (1, 0)):
                pe.wait_ge(*at("S", 2 * vi + i + 1))
                pe.wait_ge(*at("F", 2 * vi + c + 1))
                pe.wait_ge(*at("G_mm", 2 * vi + c + 1))
                if lat:
                    for hh in range(RH):
                        ins = mm(ps[c * CH:(c + 1) * CH, 0, hs[hh]], QT[:, hh, c * CH:(c + 1) * CH], state[:, dr, hh, :],
                                 start=False, stop=(i == 1), skip_group_check=True)
                    if i == 1:
                        ins.then_inc(*up("y"))
                for hh in range(RH):
                    ins = mm(ps[0:HN, 6 + c, hs[hh]], FTs[:, c, hh, :], state[:, dr, hh, :], start=False, stop=True, skip_group_check=True)
                ins.then_inc(*up("S_mm"))

        def visit_act(a, vi):
            sec, dr, tl = VISITS[vi]
            lat, nv = sec == 1, vi - 4
            act = a.activation
            a.wait_ge(*at("wl_sum", vi + 1))
            act(sgm, ex[:, 0, :], ACT.Sigmoid).then_inc(*up("sg"))
            a.wait_ge(*at("al_sum", vi + 1))
            act(av, ex[:, 1, :], ACT.Sigmoid).then_inc(*up("rate"))
            if lat:
                a.wait_ge(*at("gl", nv + 1))
                act(gt, ps[:, 2, :], ACT.Copy).then_inc(*up("gate"))
            a.wait_ge(*at("cums", vi + 1))
            a.wait_ge(*at("sg", vi + 1))
            a.wait_ge(*at("rate", vi + 1))
            act(ex[:, 0, :], ps[:, 3, :], ACT.Exp)
            act(ex[:, 1, :], ps[:, 4, :], ACT.Exp)
            act(ex[:, 2, :], ps[:, 4, :], ACT.Exp, scale=-1.0)
            act(ex[:, 3, :], ps[:, 5, :], ACT.Exp)
            act(pcs, ps[0:HN, 6, 0:16].rearrange("p (h c) -> p h c", c=2), ACT.Exp).then_inc(*up("ex"))
            for name, b, dst in (("A", 0, ART[:, :, 0, :]), ("K", 6, KT[:, :, :])):
                a.wait_ge(*at("row_tp", nth_row(vi, name)))
                act(dst, banks(b, 2)[0:HN, :].rearrange("p (h n) -> p h n", n=P), ACT.Copy).then_inc(*up("col_ak"))
            a.wait_ge(*at("X_mm", vi + 1))
            act(AX_[:, :, 1, :], heads(ps[:, 0, :]), ACT.Copy).then_inc(*up("X"))
            for l in range(NL):
                for hg in range(2):
                    a.wait_ge(*at("Z_mm", 2 * (NL * vi + l) + hg + 1))
                    act(Zs[:, 4 * hg:4 * hg + 4, :], ps[:, 2 + hg, :].rearrange("p (h n) -> p h n", n=P), ACT.Copy).then_inc(*up("Z"))
            a.wait_ge(*at("WU_mm", vi + 1))
            act(WU, banks(0, 2).rearrange("p (h n) -> p h n", n=P), ACT.Copy).then_inc(*up("WU"))
            if lat:
                a.wait_ge(*at("gn_var", nv + 1))
                act(stat[:, 48:56], stat[:, 40:48], ACT.Sqrt).then_inc(*up("gn_root"))

        def visit_pool(p, vi):
            sec, dr, tl = VISITS[vi]
            tt = p.tensor_tensor
            p.wait_ge(*at("rate", vi + 1))
            p.wait_ge(*at("kk", 2 * sec + tl + 1))
            tt(bb, tokv(tl, 3), av, ALU.mult).then_inc(*up("bb"))
            p.wait_ge(*now("bb"))
            p.wait_ge(*at("ex", vi + 1))
            tt(Bp, bb, ex[:, 3, :], ALU.mult).then_inc(*up("pool_own"))
            p.wait_ge(*now("pool_own"))
            p.wait_ge(*at("kd", vi + 1))
            tt(Kp, kd, ex[:, 3, :], ALU.mult).then_inc(*up("rem_rows"))
            p.wait_ge(*now("rem_rows"))
            p.wait_ge(*at("Mb", 2 * vi + 2))
            for l in range(NL):
                if l:
                    p.wait_ge(*at("Z_mm", 2 * (NL * vi + l)))
                tt(ME, MbT[:, :, 0, :], k_(f"lev{LEVELS[l]}").unsqueeze(1).to_broadcast([P, RH, P]), ALU.mult).then_inc(*up("ME"))
                p.wait_ge(*now("ME"))

        def visit_dve(d, vi):
            sec, dr, tl = VISITS[vi]
            lat, nv = sec == 1, vi - 4
            tt, stt = d.tensor_tensor, d.scalar_tensor_tensor
            r, k, v_, kk = (tokv(tl, i) for i in range(4))
            d.wait_ge(*at("wl", vi + 1))
            tt(ex[:, 0, :], ps[:, 0, :], w0b[:, dr, :], ALU.add).then_inc(*up("wl_sum"))
            d.wait_ge(*now("wl_sum"))
            d.wait_ge(*at("al", vi + 1))
            tt(ex[:, 1, :], ps[:, 1, :], a0b[:, dr, :], ALU.add).then_inc(*up("al_sum"))
            d.wait_ge(*now("al_sum"))
            d.wait_ge(*at("rate", vi + 1))
            stt(kd, av, -1.0, kab, ALU.add, ALU.mult).then_inc(*up("dve_own"))
            d.wait_ge(*now("dve_own"))
            stt(kd, kd, 1.0, k, ALU.add, ALU.mult).then_inc(*up("kd"))
            d.wait_ge(*now("kd"))
            d.wait_ge(*at("ex", vi + 1))
            stt(AX_[:, :, 0, :], heads(kk), -1.0, heads(ex[:, 0, :]), ALU.mult, ALU.mult).then_inc(*up("row"))
            d.wait_ge(*now("row"))
            d.wait_ge(*at("bb", vi + 1))
            tt(Bt, bb, ex[:, 2, :], ALU.mult).then_inc(*up("row"))
            d.wait_ge(*now("row"))
            tt(Kt, kd, ex[:, 2, :], ALU.mult).then_inc(*up("row"))
            d.wait_ge(*now("row"))
            if lat:
                d.wait_ge(*at("tok0", tl + 1))
                tt(Rt, r, ex[:, 1, :], ALU.mult).then_inc(*up("row"))
                d.wait_ge(*now("row"))
            for name, b, dst in (("B", 4, BT[:, :, :]), ("R", 2, ART[:, :, 1, :])):
                if name == "R" and not lat:
                    continue
                d.wait_ge(*at("row_tp", nth_row(vi, name)))
                d.tensor_copy(dst, banks(b, 2)[0:HN, :].rearrange("p (h n) -> p h n", n=P)).then_inc(*up("col_br"))
                d.wait_ge(*now("col_br"))
            wd = 2 if lat else 1
            pair = k_(f"pair{dr}").rearrange("p (a b) -> p a b", b=P)[:, 0:wd, :].unsqueeze(1).to_broadcast([P, 4, wd, P])
            every = [P, 4, P]
            for hg in range(2):
                mb, mk = ((2, 4), (6, 2))[hg]
                hq = slice(4 * hg, 4 * hg + 4)
                d.wait_ge(*at("Mb_mm", 2 * vi + hg + 1))
                tt(MbT[:, hq, 0:wd, :], banks(mb, 2)[:, 0:4 * wd * P].rearrange("p (h a b) -> p h a b", a=wd, b=P), pair, ALU.mult).then_inc(*up("Mb"))
                d.wait_ge(*now("Mb"))
                tt(Ti[:, hq, :], ps[:, hg, :].rearrange("p (h n) -> p h n", n=P), k_(f"first{dr}").unsqueeze(1).to_broadcast(every), ALU.mult).then_inc(*up("dve_own"))
                d.wait_ge(*now("dve_own"))
                d.wait_ge(*at("Mk_mm", 2 * vi + hg + 1))
                tt(MkT[:, hq, 0:wd, :], banks(mk, 2)[:, 0:4 * wd * P].rearrange("p (h a b) -> p h a b", a=wd, b=P), pair, ALU.mult).then_inc(*up("Mk"))
                d.wait_ge(*now("Mk"))
                idb = ident.unsqueeze(1).to_broadcast(every)
                tt(TiT[:, hq, :], MbT[:, hq, 0, :], k_("lev1").unsqueeze(1).to_broadcast(every), ALU.mult).then_inc(*up("dve_own"))
                d.wait_ge(*now("dve_own"))
                tt(TiT[:, hq, :], TiT[:, hq, :], idb, ALU.add).then_inc(*up("dve_own"))
                d.wait_ge(*now("dve_own"))
                tt(Ti[:, hq, :], Ti[:, hq, :], idb, ALU.add).then_inc(*up("Ti"))
                d.wait_ge(*now("Ti"))
            for l in range(NL):
                last = l == NL - 1
                for hg in range(2):
                    hq = slice(4 * hg, 4 * hg + 4)
                    d.wait_ge(*at("T_mm", 2 * (NL * vi + l) + hg + 1))
                    tt(TiT[:, hq, :], TiT[:, hq, :], ps[:, 6 + hg, :].rearrange("p (h n) -> p h n", n=P), ALU.add).then_inc(*up("TiT" if last else "dve_own"))
                    d.wait_ge(*now("TiT" if last else "dve_own"))
                    if not last:
                        tt(Ti[:, hq, :], Ti[:, hq, :], ps[:, 4 + hg, :].rearrange("p (h n) -> p h n", n=P), ALU.add).then_inc(*up("Ti"))
                        d.wait_ge(*now("Ti"))
            if lat:
                d.wait_ge(*at("Q_mm", nv + 1))
                tt(QT, ART[:, :, 1, :], banks(2, 2)[0:HN, :].rearrange("p (h n) -> p h n", n=P), ALU.add).then_inc(*up("QT"))
                d.wait_ge(*now("QT"))
            idh = k_("ident", 0, HN, HN)
            for c in range(2):
                d.wait_ge(*at("F_mm", 2 * vi + c + 1))
                for hh in range(RH):
                    ins = stt(FTs[:, c, hh, :], idh, pcs[:, hh, c:c + 1], ps[0:HN, 4 + c, hh * HN:(hh + 1) * HN], ALU.mult, ALU.add)
                ins.then_inc(*up("F"))
                d.wait_ge(*now("F"))
            for i, c in enumerate((0, 1) if dr == 0 else (1, 0)):
                d.wait_ge(*at("S_mm", 2 * vi + i + 1))
                d.tensor_copy(state[:, dr, :, :], heads(ps[0:HN, 6 + c, :])).then_inc(*up("S"))
                d.wait_ge(*now("S"))
            if not lat:
                return
            y0, y1, y2, y3 = (yo[:, i, :] for i in range(4))
            s8, m8, r8 = stat[:, 32:40], stat[:, 40:48], stat[:, 48:56]
            wide8 = lambda ap: ap.unsqueeze(2).to_broadcast([P, RH, HN])
            d.wait_ge(*at("y", nv + 1))
            d.tensor_copy(y0, ps[:, 0, :]).then_inc(*up("dve_own"))
            d.wait_ge(*now("dve_own"))
            d.tensor_reduce(s8, heads(y0), AX, ALU.add).then_inc(*up("dve_own"))
            d.wait_ge(*now("dve_own"))
            d.tensor_scalar_mul(s8, s8, 1.0 / HN).then_inc(*up("dve_own"))
            d.wait_ge(*now("dve_own"))
            tt(heads(y0), heads(y0), wide8(s8), ALU.subtract).then_inc(*up("dve_own"))
            d.wait_ge(*now("dve_own"))
            tt(y1, y0, y0, ALU.mult).then_inc(*up("dve_own"))
            d.wait_ge(*now("dve_own"))
            d.tensor_reduce(m8, heads(y1), AX, ALU.add).then_inc(*up("dve_own"))
            d.wait_ge(*now("dve_own"))
            d.tensor_scalar(m8, m8, 1.0 / HN, GN_EPS, ALU.mult, ALU.add).then_inc(*up("gn_var"))
            d.wait_ge(*now("gn_var"))
            tt(y2, r, kd, ALU.mult).then_inc(*up("dve_own"))
            d.wait_ge(*now("dve_own"))
            tt(y2, y2, rkb[:, dr, :], ALU.mult).then_inc(*up("dve_own"))
            d.wait_ge(*now("dve_own"))
            d.tensor_reduce(s8, heads(y2), AX, ALU.add).then_inc(*up("dve_own"))
            d.wait_ge(*now("dve_own"))
            tt(heads(y2), heads(v_), wide8(s8), ALU.mult).then_inc(*up("dve_own"))
            d.wait_ge(*now("dve_own"))
            d.wait_ge(*at("gn_root", nv + 1))
            d.reciprocal(r8, r8).then_inc(*up("dve_own"))
            d.wait_ge(*now("dve_own"))
            tt(heads(y0), heads(y0), wide8(r8), ALU.mult).then_inc(*up("dve_own"))
            d.wait_ge(*now("dve_own"))
            tt(y0, y0, gngb, ALU.mult).then_inc(*up("dve_own"))
            d.wait_ge(*now("dve_own"))
            tt(y0, y0, gnbb, ALU.add).then_inc(*up("dve_own"))
            d.wait_ge(*now("dve_own"))
            tt(y0, y0, y2, ALU.add).then_inc(*up("dve_own"))
            d.wait_ge(*now("dve_own"))
            if nv < 2:
                tt(rw[:, tl, :], y0, gt, ALU.mult).then_inc(*up("v_end"))
                d.wait_ge(*now("v_end"))
            else:
                tt(y0, y0, gt, ALU.mult).then_inc(*up("dve_own"))
                d.wait_ge(*now("dve_own"))
                tt(rw[:, tl, :], rw[:, tl, :], y0, ALU.add).then_inc(*up("v_end"))
                d.wait_ge(*now("v_end"))

        def rwkv(e, section, visit):
            for sec in range(2):
                section(e, sec)
                for vi in range(4 * sec, 4 * sec + 4):
                    visit(e, vi)

        def load3_pool(p):
            e = p

            def get(dst, src, name="moe_const"):
                e.dma_start(dst, src).then_inc(sems(name), 16)
            p.wait_ge(*at("v_end", 4))
            get(wr, x["w_router_2"][0].rearrange("(k p) n -> p k n", p=P))
            get(brb, x["b_router_2"][0].partition_broadcast(P))
            get(b2s, x["b2_2"][0])
            get(b1s, x["b1_2"][0].rearrange("e (a n) -> (e a) n", a=2))
            get(ln2g, x["ln2_g_2"][0].partition_broadcast(P))
            get(ln2b, x["ln2_b_2"][0].partition_broadcast(P))
            p.wait_ge(*at("catT", 2))
            get(ln1g, x["ln1_g_2"][0].partition_broadcast(P), "ln1_in")
            get(ln1b, x["ln1_b_2"][0].partition_broadcast(P), "ln1_in")
        MOE_CONST = 6 * 16
        ROWS = (16, 32, 24, 40)

        def mid_pe(pe):
            mm, tr = pe.matmul, pe.transpose
            pe.wait_ge(*at("v_end", 4))
            for tt in range(TT):
                for t in range(4):
                    ins = tr(ps[:, tt, t * P:(t + 1) * P], rw[:, tt, t * P:(t + 1) * P], ident)
                ins.then_inc(*up("rw_tp"))
            for i, t0 in enumerate(ROWS):
                b = (2, 0)[i % 2]
                if i == 1:
                    pe.wait_ge(*at("catT", 2))
                elif i >= 2:
                    pe.wait_ge(*at("rowb", i - 1))
                for t in range(KD):
                    ins = mm(banks(b, 2)[:, t * P:(t + 1) * P], modT[:, t0 + t, 0:1].to_broadcast([P, P]), ident, start=True, stop=True)
                ins.then_inc(*up("row_mm"))
            pe.wait_ge(*at("catT", 2))
            out_pe(pe, N_OUT2, catT)
            for b in range(4):
                tt, k0 = b // 2, 4 * (b % 2)
                pe.wait_ge(*at("h2", tt + 1))
                if b == 0:
                    pe.wait_ge(*at("rowb", 4))
                for k in range(4):
                    ins = tr(ps[:, b, k * P:(k + 1) * P], h2[:, tt, (k0 + k) * P:(k0 + k + 1) * P], ident)
                ins.then_inc(*up("h2_tp"))
            pe.wait_ge(*at("moe_const", MOE_CONST))
            pe.wait_ge(*at("h2T", 4))
            for tt in range(TT):
                for k in range(KD):
                    ins = mm(ps[:, 4 + tt, 0:NE], h2T[:, k, tt * P:(tt + 1) * P], wr[:, k, :], start=(k == 0), stop=(k == KD - 1))
                ins.then_inc(*up("logits"))
            for jj in range(4):
                for par in range(2):
                    i = 2 * jj + par
                    ins = tr(ps[:, 0, i * 2 * NE:(i + 1) * 2 * NE], b1s[:, jj * 2 * P + par:(jj + 1) * 2 * P:2], k_("ident", 0, 2 * NE, 2 * NE))
            ins.then_inc(*up("b1_tp"))
            pe.wait_ge(*at("mask", TT))
            mm(ps[:, 6, 0:NE], k_("earlier"), mask[:, 0, :], start=True, stop=True)
            mm(ps[:, 6, NE:2 * NE], k_("ones"), mask[:, 0, :], start=True, stop=False)
            mm(ps[:, 6, NE:2 * NE], k_("earlier"), mask[:, 1, :], start=False, stop=True)
            mm(ps[:, 6, 2 * NE:3 * NE], k_("ones"), mask[:, 0, :], start=True, stop=False)
            mm(ps[:, 6, 2 * NE:3 * NE], k_("ones"), mask[:, 1, :], start=False, stop=True).then_inc(*up("rank_mm"))
            pe.wait_ge(*at("gw", TT))
            for tt in range(TT):
                ins = tr(ps[0:NE, 7, tt * P:(tt + 1) * P], gw[:, tt, 0:NE], ident)
            ins.then_inc(*up("gw_tp"))
            pe.wait_ge(*at("GT", 1))
            pe.wait_ge(*at("b1T", 1))
            for tt in range(TT):
                for nh in range(2):
                    ins = mm(ps[:, 2 * tt + nh, :], GT[:, tt * P:(tt + 1) * P], b2s[:, nh * 512:(nh + 1) * 512], start=True, stop=True)
                ins.then_inc(*up("acc_mm"))

        def mid_act(a):
            act = a.activation
            for tt in range(TT):
                a.wait_ge(*at("rw_tp", tt + 1))
                act(catT[:, 0:4, tt * P:(tt + 1) * P], ps[:, tt, :].rearrange("p (a b) -> p a b", b=P), ACT.Copy).then_inc(*up("catT"))
            for i in range(4):
                a.wait_ge(*at("row_mm", i + 1))
                act(rowb[:, i, :], banks((2, 0)[i % 2], 2), ACT.Copy).then_inc(*up("rowb"))
            ln_act(a, 2, 2)
            for tt in range(TT):
                a.wait_ge(*at("top", tt + 1))
                act(ek[:, tt, 0:TOPK], top[:, tt, 0:TOPK], ACT.Exp, bias=stat[:, 16 + tt:17 + tt], accum_out=stat[:, 18 + tt:19 + tt]).then_inc(*up("ek"))
                a.wait_ge(*now("ek"))

        def mid_dve(d):
            tt_, stt, ts = d.tensor_tensor, d.scalar_tensor_tensor, d.tensor_scalar
            d.wait_ge(*at("w_used", N_OUT2 + 3))
            d.wait_ge(*at("rowb", 4))
            for tt in range(TT):
                tt_(tmpx[:, tt, :], banks(4 + 2 * tt, 2), rowb[:, 0, :], ALU.mult).then_inc(*up("dve_own"))
                d.wait_ge(*now("dve_own"))
                stt(tmpx[:, tt, :], h[:, tt, :], DEEP, tmpx[:, tt, :], ALU.mult, ALU.add).then_inc(*up("dve_own"))
                d.wait_ge(*now("dve_own"))
            d.wait_ge(*at("ln1_in", 32))
            ln_dve(d, 2, [tmpx[:, 0, :], tmpx[:, 1, :]], [h[:, 0, :], h[:, 1, :]], ln1g, ln1b)
            for tt in range(TT):
                tt_(h2[:, tt, :], h[:, tt, :], rowb[:, 1, :], ALU.mult).then_inc(*up("dve_own"))
                d.wait_ge(*now("dve_own"))
                tt_(h2[:, tt, :], h2[:, tt, :], rowb[:, 2, :], ALU.add).then_inc(*up("h2"))
                d.wait_ge(*now("h2"))
            for b in range(4):
                tt, k0 = b // 2, 4 * (b % 2)
                d.wait_ge(*at("h2_tp", b + 1))
                d.tensor_copy(h2T[:, k0:k0 + 4, tt * P:(tt + 1) * P], ps[:, b, :].rearrange("p (a b) -> p a b", b=P)).then_inc(*up("h2T"))
                d.wait_ge(*now("h2T"))
            d.wait_ge(*at("moe_const", MOE_CONST))
            count32 = k_("slots", 0, NE)
            d.memset(rk[:, :, NE:NE + 1], -1.0).then_inc(*up("dve_own"))
            d.wait_ge(*now("dve_own"))
            d.memset(gw[:, :, NE:NE + 1], 0.0).then_inc(*up("dve_own"))
            d.wait_ge(*now("dve_own"))
            d.memset(b1T[:, :, NE:NE + 1], 0.0).then_inc(*up("dve_own"))
            d.wait_ge(*now("dve_own"))
            for tt in range(TT):
                d.wait_ge(*at("logits", tt + 1))
                tt_(lg[:, tt, :], ps[:, 4 + tt, 0:NE], brb, ALU.add).then_inc(*up("dve_own"))
                d.wait_ge(*now("dve_own"))
                d.max(top[:, tt, :], lg[:, tt, :]).then_inc(*up("dve_own"))
                d.wait_ge(*now("dve_own"))
                d.max_index(idx[:, tt, :], top[:, tt, :], lg[:, tt, :]).then_inc(*up("dve_own"))
                d.wait_ge(*now("dve_own"))
                d.tensor_scalar_mul(stat[:, 16 + tt:17 + tt], top[:, tt, 0:1], -1.0).then_inc(*up("top"))
                d.wait_ge(*now("top"))
                d.tensor_copy(idxf[:, tt, :], idx[:, tt, :]).then_inc(*up("dve_own"))
                d.wait_ge(*now("dve_own"))
                ts(mask[:, tt, :], count32, idxf[:, tt, 0:1], None, ALU.is_equal).then_inc(*up("dve_own"))
                d.wait_ge(*now("dve_own"))
                for k in range(1, TOPK):
                    stt(mask[:, tt, :], count32, idxf[:, tt, k:k + 1], mask[:, tt, :], ALU.is_equal, ALU.add).then_inc(*up("mask" if k == TOPK - 1 else "dve_own"))
                    d.wait_ge(*now("mask" if k == TOPK - 1 else "dve_own"))
                d.wait_ge(*at("ek", tt + 1))
                d.reciprocal(stat[:, 20 + tt:21 + tt], stat[:, 18 + tt:19 + tt]).then_inc(*up("dve_own"))
                d.wait_ge(*now("dve_own"))
                ts(ek[:, tt, 0:TOPK], ek[:, tt, 0:TOPK], stat[:, 20 + tt:21 + tt], None, ALU.mult).then_inc(*up("dve_own"))
                d.wait_ge(*now("dve_own"))
                ts(gw[:, tt, 0:NE], count32, idxf[:, tt, 0:1], ek[:, tt, 0:1], ALU.is_equal, ALU.mult).then_inc(*up("dve_own"))
                d.wait_ge(*now("dve_own"))
                for k in range(1, TOPK):
                    ts(hot32, count32, idxf[:, tt, k:k + 1], ek[:, tt, k:k + 1], ALU.is_equal, ALU.mult).then_inc(*up("dve_own"))
                    d.wait_ge(*now("dve_own"))
                    tt_(gw[:, tt, 0:NE], gw[:, tt, 0:NE], hot32, ALU.add).then_inc(*up("gw" if k == TOPK - 1 else "dve_own"))
                    d.wait_ge(*now("gw" if k == TOPK - 1 else "dve_own"))
            d.wait_ge(*at("b1_tp", 1))
            for half in range(2):
                src = ps[:, 0, :].rearrange("p (i e a) -> p i e a", e=NE, a=2)[:, :, :, half]
                d.tensor_copy(b1T[:, 8 * half:8 * half + 8, 0:NE], src).then_inc(*up("b1T" if half else "dve_own"))
                d.wait_ge(*now("b1T" if half else "dve_own"))
            d.wait_ge(*at("rank_mm", 1))
            for tt in range(TT):
                stt(rk[:, tt, 0:NE], ps[:, 6, tt * NE:(tt + 1) * NE], 1.0, mask[:, tt, :], ALU.add, ALU.mult).then_inc(*up("dve_own"))
                d.wait_ge(*now("dve_own"))
                d.tensor_scalar_add(rk[:, tt, 0:NE], rk[:, tt, 0:NE], -1.0).then_inc(*up("dve_own"))
                d.wait_ge(*now("dve_own"))
            d.tensor_reduce(stat[0:1, 61:62], ps[0:1, 6, 2 * NE:3 * NE], AX, ALU.max).then_inc(*up("dve_own"))
            d.wait_ge(*now("dve_own"))
            d.tensor_copy(cnt[0:1, NE:NE + 1], stat[0:1, 61:62])
            d.tensor_copy(cnt[0:1, 0:NE], ps[0:1, 6, 2 * NE:3 * NE]).then_inc(*up("cnt"))
            d.wait_ge(*now("cnt"))
            d.wait_ge(*at("gw_tp", 1))
            d.tensor_copy(GT, ps[0:NE, 7, 0:S]).then_inc(*up("GT"))
            d.wait_ge(*now("GT"))
            for tt in range(TT):
                d.wait_ge(*at("acc_mm", tt + 1))
                d.tensor_copy(acc[:, tt, :], banks(2 * tt, 2)).then_inc(*up("acc0"))
                d.wait_ge(*now("acc0"))
            d.memset(MAIN[3], 0.0).then_inc(*up("dve_own"))
            d.wait_ge(*now("dve_own"))
            d.memset(MAIN[4], 0.0).then_inc(*up("acc0"))
            d.wait_ge(*now("acc0"))

        def w1_slot(j):
            return ring[:, j, 0:2048].rearrange("p (k n) -> p k n", k=KD)

        def moe_sync(e, turns):
            def load(i, j):
                e.dma_start(w1_slot(j), x["w1_2"][0, bass.ds(i, 1), :, j * 2 * P:(j + 1) * 2 * P].rearrange("a (k p) n -> p (a k) n", p=P)).then_inc(sems(f"w_landed{j}"), 16)
                e.dma_start(ring[:, j, 2048:3072], x["w2_2"][0, bass.ds(i, 1), j * P:(j + 1) * P, :].rearrange("a p n -> p (a n)")).then_inc(sems(f"w_landed{j}"), 16)

            with e.Fori(0, NE) as i:
                for j in range(EJ):
                    e.wait_ge(*at("w_used", i * EJ + (N_MOE + j - RING + 1)))
                    load(i, j)

            def more(i, b, n):
                e.wait_ge(*at("w_used", n + (NE * EJ + N_MOE)))
                for j in range(EJ):
                    load(i, j)
            e.wait_ge(*at("cnt", 1))
            moe_more(e, turns, more)

        def moe_landed(e, i, j):
            e.wait_ge(*at(f"w_landed{j}", i * 32 + (per_slot[j] + 32)))

        def gather_pe(pe, buf, bank, gathered):
            sel, selg = buf[0], buf[1]
            for k in range(KD):
                for tt in range(TT):
                    ins = pe.matmul(banks(bank, 2)[:, k * BS:(k + 1) * BS], h2[:, tt, k * P:(k + 1) * P], sel[:, tt, :], start=(tt == 0), stop=(tt == 1))
            ins.then_inc(sems(gathered), 1)

        def select_tp_pe(pe, buf, bank, name):
            for tt in range(TT):
                ins = pe.matmul(ps[0:BS, bank, tt * P:(tt + 1) * P], buf[1][:, tt, :], ident, start=True, stop=True)
            ins.then_inc(sems(name), 1)

        def up_pe(pe, buf, j, name):
            w = w1_slot(j)
            for par in range(2):
                for k in range(KD):
                    ins = pe.matmul(ps[:, 2 + j % 2, par * BS:(par + 1) * BS], w[:, k, par:2 * P:2], buf[2][:, k, :],
                                        start=(k == 0), stop=(k == KD - 1))
            ins.then_inc(sems(name), 1)

        def down_pe(pe, j, name):
            for nh in range(2):
                ins = pe.matmul(ps[0:BS, 4 + nh, :], acts[:, j % 2, :], ring[:, j, 2048 + nh * 512:2048 + (nh + 1) * 512],
                                    start=(j == 0), stop=(j == EJ - 1))
            if name:
                ins.then_inc(sems(name), 1)

        def scatter_pe(pe, buf, name):
            for tt in range(TT):
                for nh in range(2):
                    ins = pe.matmul(ps[:, (6, 0)[tt] + nh, :], buf[3][:, tt * P:(tt + 1) * P], buf[4][:, nh * 512:(nh + 1) * 512], start=True, stop=True)
                ins.then_inc(sems(name), 1)

        def moe_more(e, turns, body):
            most = e.value_load(cnt[0:1, NE:NE + 1], min_val=0, max_val=S)
            with e.If(most > BS):
                with e.Fori(0, NE) as i:
                    c = e.value_load(cnt[0:1, bass.ds(i, 1)], min_val=0, max_val=S)
                    with e.Fori(1, S // BS) as b:
                        with e.If(c > b * BS):
                            n = e.snap(turns)
                            body(i, b, n)
                            e.reg_add(turns, turns, 1)

        def moe_pe(pe, turns):
            pe.wait_ge(*at("acc0", 3))
            pe.wait_ge(*at("sel", 1))
            gather_pe(pe, MAIN, 0, "gathered")
            pe.wait_ge(*at("xs", 1))
            with pe.Fori(0, NE) as i:
                for j in range(EJ + 1):
                    if j < EJ:
                        moe_landed(pe, i, j)
                        up_pe(pe, MAIN, j, "up")
                    if j == 0:
                        pe.wait_ge(*at("ys", i + 1))
                        scatter_pe(pe, MAIN, "scat")
                    if j == 2:
                        pe.wait_ge(*at("acc", i * 2 + 2))
                        select_tp_pe(pe, MAIN, 1, "sel_tp")
                    if j == EJ:
                        pe.wait_ge(*at("sgt", i + 1))
                        pe.wait_ge(*at("sel", i + 2))
                        gather_pe(pe, MAIN, 0, "gathered")
                    if j:
                        pe.wait_ge(*at("act", i * EJ + j))
                        down_pe(pe, j - 1, "w_used")
                pe.wait_ge(*at("xs", i + 2))
            pe.wait_ge(*at("ys", NE + 1))
            scatter_pe(pe, MAIN, "scat")
            pe.wait_ge(*at("acc", NE * 2 + 2))

            def more(i, b, n):
                pe.wait_ge(*at("sel2", n + 1))
                gather_pe(pe, MORE, 0, "gathered2")
                select_tp_pe(pe, MORE, 2, "sel_tp2")
                pe.wait_ge(*at("xs2", n + 1))
                pe.wait_ge(*at("sgt2", n + 1))
                for j in range(EJ + 1):
                    if j < EJ:
                        moe_landed(pe, n + NE, j)
                        up_pe(pe, MORE, j, "up2")
                    if j:
                        pe.wait_ge(*at("act2", n * EJ + j))
                        down_pe(pe, j - 1, "w_used" if j == EJ else None)
                pe.wait_ge(*at("ys2", n + 1))
                scatter_pe(pe, MORE, "scat2")
                pe.wait_ge(*at("acc2", n * 2 + 2))
            moe_more(pe, turns, more)

        def moe_act(a, turns):
            act = a.activation
            xs_bank = banks(0, 2)[:, 0:KD * BS].rearrange("p (k n) -> p k n", k=KD)

            def hidden(j, n, glu_, sig_):
                a.wait_ge(*at(glu_, n))
                act(sig[:, j % 2, :], glu[:, j % 2, :], ACT.Sigmoid, scale=1.702).then_inc(sems(sig_), 1)

            a.wait_ge(*at("gathered", 1))
            act(MAIN[2], xs_bank, ACT.Copy).then_inc(sems("xs"), 1)
            act(stat[:, 62:63], stat[:, 0:1], ACT.Copy).then_inc(sems("ys"), 1)
            with a.Fori(0, NE) as i:
                for j in range(EJ):
                    if j == 3:
                        a.wait_ge(*at("sel_tp", i + 1))
                        act(MAIN[3], ps[0:BS, 1, 0:S], ACT.Copy).then_inc(sems("sgt"), 1)
                    hidden(j, i * EJ + (j + 1), "glu", "sig")
                a.wait_ge(*at("gathered", i + 2))
                a.wait_ge(*at("up", i * EJ + EJ))
                act(MAIN[2], xs_bank, ACT.Copy).then_inc(sems("xs"), 1)
                a.wait_ge(*at("w_used", i * EJ + (N_MOE + EJ)))
                a.wait_ge(*at("scat", i * 2 + 2))
                act(MAIN[4], banks(4, 2)[0:BS, :], ACT.Copy).then_inc(sems("ys"), 1)

            def more(i, b, n):
                a.wait_ge(*at("gathered2", n + 1))
                act(MORE[2], xs_bank, ACT.Copy).then_inc(sems("xs2"), 1)
                a.wait_ge(*at("sel_tp2", n + 1))
                act(MORE[3], ps[0:BS, 2, 0:S], ACT.Copy).then_inc(sems("sgt2"), 1)
                for j in range(EJ):
                    hidden(j, n * EJ + (j + 1), "glu2", "sig2")
                a.wait_ge(*at("w_used", n + (NE * EJ + N_MOE + 1)))
                act(MORE[4], banks(4, 2)[0:BS, :], ACT.Copy).then_inc(sems("ys2"), 1)
            moe_more(a, turns, more)

        def moe_dve(d, turns):
            ts, stt, tt_ = d.tensor_scalar, d.scalar_tensor_tensor, d.tensor_tensor
            own = [0]

            def columns(i, c):
                d.tensor_copy(rke, rk[:, :, bass.ds(i, 1)].rearrange("p a b -> p (a b)"))
                d.tensor_copy(gwe, gw[:, :, bass.ds(i, 1)].rearrange("p a b -> p (a b)")).then_inc(sems("cols_e"), 1)
                d.wait_ge(*at("cols_e", c))

            def select(buf, b, name):
                first = k_("slots", 0, BS) if b is None else const[:, bass.ds(b * BS + CONST_AT["slots"][0], BS)]
                for tt in range(TT):
                    ts(buf[0][:, tt, :], first, rke[:, tt:tt + 1], None, ALU.is_equal)
                    ins = ts(buf[1][:, tt, :], first, rke[:, tt:tt + 1], gwe[:, tt:tt + 1], ALU.is_equal, ALU.mult)
                ins.then_inc(sems(name), 1)

            def hidden(j, n, up, glu_, lin_, sig_, act_):
                a, b = glu[:, j % 2, :], lin[:, j % 2, :]
                d.wait_ge(*at(up, n))
                src = ps[:, 2 + j % 2, :]
                ts(a, src[:, 0:BS], b1e[:, 2 * j:2 * j + 1], LIMIT, ALU.add, ALU.min).then_inc(sems(glu_), 1)
                ts(b, src[:, BS:2 * BS], b1e[:, 2 * j + 1:2 * j + 2], LIMIT, ALU.add, ALU.min).then_inc(sems(lin_), 1)
                d.wait_ge(*at(lin_, n * 3 - 2))
                ts(b, b, -LIMIT, 1.0, ALU.max, ALU.add).then_inc(sems(lin_), 1)
                d.wait_ge(*at(lin_, n * 3 - 1))
                tt_(b, b, a, ALU.mult).then_inc(sems(lin_), 1)
                d.wait_ge(*at(lin_, n * 3))
                d.wait_ge(*at(sig_, n))
                tt_(acts[:, j % 2, :], b, sig[:, j % 2, :], ALU.mult).then_inc(sems(act_), 1)

            def add(tt, scat, acc_, n):
                d.wait_ge(*at(scat, n))
                tt_(acc[:, tt, :], acc[:, tt, :], banks((6, 0)[tt], 2), ALU.add).then_inc(sems(acc_), 1)

            columns(0, 1)
            select(MAIN, None, "sel")
            with d.Fori(0, NE) as i:
                d.tensor_copy(b1e, b1T[:, :, bass.ds(i, 1)].rearrange("p a b -> p (a b)")).then_inc(sems("b1e"), 1)
                d.wait_ge(*at("b1e", i + 1))

                for j in range(EJ):
                    hidden(j, i * EJ + (j + 1), "up", "glu", "lin", "sig", "act")
                    if j == 0:
                        for tt in range(TT):
                            add(tt, "scat", "acc", i * 2 + (tt + 1))
                    if j == 5:
                        d.wait_ge(*at("sel_tp", i + 1))
                        columns(i + 1, i + 2)
                        select(MAIN, None, "sel")
            for tt in range(TT):
                add(tt, "scat", "acc", NE * 2 + tt + 1)
            d.wait_ge(*at("acc", NE * 2 + TT))

            def more(i, b, n):
                columns(i, n + (NE + 2))
                d.tensor_copy(b1e, b1T[:, :, bass.ds(i, 1)].rearrange("p a b -> p (a b)")).then_inc(sems("b1e"), 1)
                d.wait_ge(*at("b1e", n + (NE + 1)))
                select(MORE, b, "sel2")
                for j in range(EJ):
                    hidden(j, n * EJ + (j + 1), "up2", "glu2", "lin2", "sig2", "act2")
                for tt in range(TT):
                    add(tt, "scat2", "acc2", n * 2 + (tt + 1))
                d.wait_ge(*at("acc2", n * 2 + TT))
            moe_more(d, turns, more)
            for tt in range(TT):
                tt_(acc[:, tt, :], acc[:, tt, :], rowb[:, 3, :], ALU.mult).then_inc(*up("dve_own"))
                d.wait_ge(*now("dve_own"))
                stt(acc[:, tt, :], h[:, tt, :], DEEP, acc[:, tt, :], ALU.mult, ALU.add).then_inc(*up("dve_own"))
                d.wait_ge(*now("dve_own"))
            ln_dve(d, 3, [acc[:, 0, :], acc[:, 1, :]], [acc[:, 0, :], acc[:, 1, :]], ln2g, ln2b)

        block = ctx.enter_context(nc.Block())

        def load_rows(e, which, name_in):
            for name, n in which:
                at_ = COL_AT[name]
                src = x[name]
                if len(src.shape) == 3:
                    src = src.rearrange("a b c -> (a b c)")
                elif len(src.shape) == 2:
                    src = src.rearrange("a b -> (a b)")
                e.dma_start(rows[at_ % P:at_ % P + n, at_ // P, :], src.rearrange("(r c) -> r c", c=P)).then_inc(sems(name_in), 16)

        @block.sync
        def _(e):
            e.dma_start(h[:, :, :], x["x"][0].rearrange("(t p) n -> p t n", p=P)).then_inc(sems("x_in"), 16)
            for n in range(N_MOE):
                send(e, n)
            turns = e.alloc_register("further_blocks_sp")
            e.reg_mov(turns, 0)
            moe_sync(e, turns)
            for tt in range(TT):
                e.wait_ge(*at("ln_x", 7 + tt))
                e.dma_start(out[0, tt * P:(tt + 1) * P, :], acc[:, tt, :]).then_inc(sems("out_done"), 16)
            e.wait_ge(*at("out_done", 16 * TT))

        @block.scalar
        def _(a):
            a.dma_start(ident, x["const"][:, 0:P]).then_inc(sems("const_in"), 16)
            load_rows(a, COLUMN_ROWS[0:ROWS_ACT], "rows_in_a")
            a.wait_ge(*at("x_in", 16))
            a.dma_start(const[:, P:NCONST], x["const"][:, P:NCONST]).then_inc(sems("const_rest"), 16)
            ffn_act(a, "f1", lambda tt: ("x_in", 16))
            post_act(a, "p1", ("w_used", N_FFN1 + FT))
            pre_act(a, "mix", lambda tt: ("post_h", nth(POSTS, "p1", 2, tt + 1)))
            a.wait_ge(*at("cols", 2))
            softplus_act(a)
            qkv_out(a, lambda o, i: a.activation(o, i, ACT.Copy), 0)
            attn_act(a)
            rec_act(a)
            post_act(a, "pm", ("w_used", N_OUT + 3))
            in2_act(a)
            ffn_act(a, "f2", lambda tt: ("post_h", nth(POSTS, "pm", 2, tt + 1)))
            post_act(a, "p2", ("w_used", N_IN2))
            ln_act(a, 1, 4)
            in2_shift_act(a)
            fourier_act(a)
            rwkv(a, section_act, visit_act)
            mid_act(a)
            turns = a.alloc_register("further_blocks_a")
            a.reg_mov(turns, 0)
            a.wait_ge(*at("cnt", 1))
            moe_act(a, turns)
            ln_act(a, 3, 2)

        @block.vector
        def _(d):
            setup_dve(d)
            d.wait_ge(*at("x_in", 16))
            ffn_dve(d, "f1", "ffn1_norm_pre", lambda j: bias_dve(d, j - 4))
            post_dve(d, "p1", 0.5)
            pre_dve(d, "mix", "mix_norm_pre")
            qkv_out(d, d.tensor_copy, 1)
            attn_dve(d)
            rec_dve(d)
            post_dve(d, "pm", 1.0)
            ffn_dve(d, "f2", "ffn2_norm_pre", lambda j: ada_dve(d, j))
            post_dve(d, "p2", 0.5)
            in2_dve(d)
            d.wait_ge(*at("in2_const", IN2_CONST))
            d.wait_ge(*at("fno", 4))
            d.memset(state, 0.0).then_inc(*up("S"))
            d.wait_ge(*now("S"))
            rwkv(d, section_dve, visit_dve)
            mid_dve(d)
            turns = d.alloc_register("further_blocks_d")
            d.reg_mov(turns, 0)
            d.wait_ge(*at("cnt", 1))
            moe_dve(d, turns)

        @block.gpsimd
        def _(p):
            load_rows(p, COLUMN_ROWS[ROWS_ACT:], "rows_in_p")
            p.dma_start(hot[:, :], x["hot"]).then_inc(sems("hot_in"), 16)
            p.dma_start(maskb[:, :], x["mask"][0].partition_broadcast(P)).then_inc(sems("hot_in"), 16)
            p.dma_start(table_sb[:, :], x["rel_bias_table"]).then_inc(sems("hot_in"), 16)
            for i, (name, tag) in enumerate((("ffn1_norm_post", "p0"), ("mix_norm_post", "p1"), ("ffn2_norm_post", "pm"))):
                if i:
                    p.wait_ge(*at("post_free", nth(POSTS, tag, 2, 2)))
                p.dma_start(post[:, :], x[name][0].partition_broadcast(P)).then_inc(sems("post_in"), 16)
                if i == 0:
                    setup_pool(p)
            load2_pool(p)
            in2_pool(p)
            rwkv(p, lambda e, sec: None, visit_pool)
            load3_pool(p)

        @block.tensor
        def _(pe):
            setup_pe(pe)
            ffn_pe(pe, "f1", lambda j: bias_pe(pe, j - 4))
            pe.wait_ge(*at("const_rest", 16))
            qkv_pe(pe)
            attn_pe(pe)
            rec_pe(pe)
            ffn_pe(pe, "f2", lambda j: ada_pe(pe, j))
            in2_pe(pe)
            fourier_pe(pe)
            pe.wait_ge(*at("in2_const", IN2_CONST))
            pe.wait_ge(*at("lora", 2))
            pe.wait_ge(*at("fno", 4))
            rwkv(pe, section_pe, visit_pe)
            mid_pe(pe)
            turns = pe.alloc_register("further_blocks_pe")
            pe.reg_mov(turns, 0)
            pe.wait_ge(*at("cnt", 1))
            moe_pe(pe, turns)


INPUTS = ("x", "ffn1_norm_pre", "ffn1_norm_post", "ffn1_w_gate", "ffn1_w_up", "ffn1_w_down", "mix_norm_pre",
          "mix_norm_post", "w_in", "rel_bias_table", "conv_w", "conv_b", "lru_w_x", "lru_b_x", "lru_w_a", "lru_b_a",
          "lru_a_param", "w_attn_branch", "w_rec_branch", "w_out", "ffn2_norm_pre", "ffn2_norm_post", "ffn2_w_gate",
          "ffn2_w_up", "ffn2_w_down", "c_2", "ctx_2", "c_ctx_2", "ln0_g_2", "ln0_b_2", "w_ada_2", "b_ada_2", "w_in_2",
          "mu_shift_2", "w0_2", "w2_decay_2", "a0_2", "a2_iclr_2", "g2_gate_2", "r_k_2", "k_k_2", "k_a_2", "gn_g_2",
          "gn_b_2", "w_fno_2", "b_fno_2", "w_out_2", "ln1_g_2", "ln1_b_2", "w_router_2", "b_router_2", "w1_2", "b1_2",
          "w2_2", "b2_2", "ln2_g_2", "ln2_b_2")


def kernel(**inputs):
    import concourse.bacc as bacc
    from concourse.bass_utils import run_bass_kernel_spmd

    nc = bacc.Bacc("TRN2", target_bir_lowering=False, num_devices=1)
    arrays = {name: np.ascontiguousarray(inputs[name]) for name in INPUTS}
    arrays.update(const=CONST_BLOB, hot=BIAS_HOT, mask=BIAS_MASK)
    given = {name: nc.dram_tensor("in_" + name, a.shape, mybir.dt.from_np(a.dtype), kind="ExternalInput").ap()
             for name, a in arrays.items()}
    out = nc.dram_tensor("out", (1, S, D), F32, kind="ExternalOutput").ap()
    build(nc, given, out)
    res = run_bass_kernel_spmd(nc, [{"in_" + name: a for name, a in arrays.items()}], core_ids=[0])
    return res.results[0]["out"]
```
